# Optimizing a Trainium2 kernel written in Bass

```python
import jax, jax.numpy as jnp
from jax import lax
import numpy as np

D_MODEL = 1024
BATCH = 1
SEQ = 256
DEPTH = 2
DEC_BATCH = 8
DEC_SEQ = 8
PAST_LEN = 2048
PAGE_SIZE = 128

A_HEADS = 8
A_DK = 128
A_DV = D_MODEL // A_HEADS
A_WIDTH_K = A_HEADS * A_DK
A_WIDTH_V = A_HEADS * A_DV
B_HEADS = 4
B_WIDTH = D_MODEL
B_DH = B_WIDTH // B_HEADS
QK_BLOCK = 4
N_QK_BLOCKS = B_WIDTH // QK_BLOCK
CONV_W = 4
CHUNK = 32
D_FF = 2816
N_EXPERTS = 8
TOP_K = 2
N_DENSE = (DEPTH + 1) // 2
N_MOE = DEPTH // 2
ALPHA = (2 * DEPTH) ** 0.25
BETA = (8 * DEPTH) ** -0.25
EPS = 1e-5
NEG = -1e30
TINY = 1e-30
IN_SIZES = (A_WIDTH_K, A_WIDTH_K, A_WIDTH_V, A_WIDTH_V, B_WIDTH, B_WIDTH, B_WIDTH, B_HEADS, B_HEADS, D_MODEL, D_MODEL)
N_IN = sum(IN_SIZES)

kernel_name = 'hgrn2_mlstm_gated_parallel_deepnorm_moe_step'

def _split_points():
    pts, acc = [], 0
    for s in IN_SIZES[:-1]:
        acc += s
        pts.append(acc)
    return tuple(pts)

def layer_norm(x, g, b):
    xf = x.astype(jnp.float32)
    mu = jnp.mean(xf, -1, keepdims=True)
    xc = xf - mu
    var = jnp.mean(xc * xc, -1, keepdims=True)
    return (xc * lax.rsqrt(var + EPS) * g + b).astype(x.dtype)

def rms_norm_heads(x, g):
    return x * lax.rsqrt(jnp.mean(x * x, -1, keepdims=True) + EPS) * g

def layer_norm_heads(x, g):
    xc = x - jnp.mean(x, -1, keepdims=True)
    return xc * lax.rsqrt(jnp.mean(xc * xc, -1, keepdims=True) + EPS) * g

def chunk_len(l):
    return CHUNK if l % CHUNK == 0 else l

def to_chunks(t, c):
    b, l = t.shape[:2]
    t = t.reshape((b, l // c, c) + t.shape[2:])
    return jnp.moveaxis(t, (1, 2), (0, 3))

def from_chunks(t):
    n, b, h, c, d = t.shape
    return jnp.moveaxis(t, (0, 3), (1, 2)).reshape(b, n * c, h, d)

def hgrn2_scan(q, k, log_f, v, s0):
    c = chunk_len(q.shape[1])
    causal = jnp.tril(jnp.ones((c, c), bool))

    def step(s, inp):
        qi, ki, gi, vi = inp
        G = jnp.cumsum(gi, axis=2)
        expo = G[:, :, :, None, :] - G[:, :, None, :, :]
        w = jnp.exp(jnp.where(causal[:, :, None], expo, NEG))
        att = jnp.einsum('bhtd,bhsd,bhtsd->bhts', qi, ki, w)
        o = jnp.einsum('bhts,bhsv->bhtv', att, vi) + jnp.einsum('bhtd,bhdv->bhtv', qi * jnp.exp(G), s)
        g_last = G[:, :, -1:, :]
        s_new = jnp.exp(g_last[:, :, 0, :])[..., None] * s + jnp.einsum('bhsd,bhsv->bhdv', ki * jnp.exp(g_last - G), vi)
        return s_new, o

    s_fin, oc = lax.scan(step, s0, (to_chunks(q, c), to_chunks(k, c), to_chunks(log_f, c), to_chunks(v, c)))
    return from_chunks(oc), s_fin

def mlstm_scan(q, k, v, i_pre, log_fg, c0, n0, m0):
    c = chunk_len(q.shape[1])
    causal = jnp.tril(jnp.ones((c, c), bool))

    def step(carry, inp):
        C, n, m = carry
        qi, ki, vi, ii, fi = inp
        b = jnp.cumsum(fi, axis=-1)
        d_intra = jnp.where(causal, b[..., :, None] - b[..., None, :] + ii[..., None, :], NEG)
        d_inter = b + m[..., None]
        m_t = jnp.maximum(jnp.max(d_intra, -1), d_inter)
        w = jnp.exp(d_intra - m_t[..., None])
        w_inter = jnp.exp(d_inter - m_t)
        s = jnp.einsum('bhtd,bhsd->bhts', qi, ki) * w
        num = jnp.einsum('bhts,bhsv->bhtv', s, vi) + w_inter[..., None] * jnp.einsum('bhtd,bhdv->bhtv', qi, C)
        den = jnp.sum(s, -1) + w_inter * jnp.einsum('bhtd,bhd->bht', qi, n)
        h = num / jnp.maximum(jnp.abs(den), jnp.exp(-m_t))[..., None]
        m_new = m_t[..., -1]
        w_state = jnp.exp(b[..., -1:] - b + ii - m_new[..., None])
        decay = jnp.exp(b[..., -1] + m - m_new)
        C_new = decay[..., None, None] * C + jnp.einsum('bhs,bhsd,bhsv->bhdv', w_state, ki, vi)
        n_new = decay[..., None] * n + jnp.einsum('bhs,bhsd->bhd', w_state, ki)
        return (C_new, n_new, m_new), h

    (c_f, n_f, m_f), hc = lax.scan(step, (c0, n0, m0), (to_chunks(q, c), to_chunks(k, c), to_chunks(v, c), to_chunks(i_pre, c), to_chunks(log_fg, c)))
    return from_chunks(hc), c_f, n_f, m_f

def causal_conv(u, buf, w, bias):
    xp = jnp.concatenate([buf.astype(u.dtype), u], axis=1)
    l = u.shape[1]
    y = sum(xp[:, j:j + l] * w[j] for j in range(CONV_W)) + bias
    return y, xp[:, -(CONV_W - 1):]

def token_mixer(x, s_hgrn, c_m, n_m, m_m, conv_buf, w_in, lb, a_norm_g, w_pa, conv_w, conv_b,
                w_q_blk, w_k_blk, b_ig, b_fg, b_norm_g, w_pb, w_o):
    f32 = jnp.float32
    bsz, seq, _ = x.shape
    z = x @ w_in
    aq, af, ai, ag, bu, bv, bo, big, bfg, ga, gb = jnp.split(z, _split_points(), axis=-1)
    lbh = lb.reshape(A_HEADS, A_DK)
    fp = af.astype(f32).reshape(bsz, seq, A_HEADS, A_DK)
    f_gate = lbh + (1.0 - lbh) * jax.nn.sigmoid(fp)
    log_f = jnp.log(jnp.maximum(f_gate, TINY))
    key_a = (1.0 - lbh) * jax.nn.sigmoid(-fp)
    q_a = jax.nn.silu(aq.astype(f32)).reshape(bsz, seq, A_HEADS, A_DK)
    v_a = ai.astype(f32).reshape(bsz, seq, A_HEADS, A_DV)
    o_a, s_new = hgrn2_scan(q_a, key_a, log_f, v_a, s_hgrn.astype(f32))
    o_a = rms_norm_heads(o_a, a_norm_g.reshape(A_HEADS, A_DV)) * jax.nn.silu(ag.astype(f32)).reshape(bsz, seq, A_HEADS, A_DV)
    y_a = o_a.reshape(bsz, seq, A_WIDTH_V).astype(x.dtype) @ w_pa
    u, conv_new = causal_conv(bu, conv_buf, conv_w, conv_b)
    u = jax.nn.silu(u).reshape(bsz, seq, N_QK_BLOCKS, QK_BLOCK)
    q_b = jnp.einsum('blni,nij->blnj', u, w_q_blk).reshape(bsz, seq, B_HEADS, B_DH).astype(f32)
    k_b = jnp.einsum('blni,nij->blnj', u, w_k_blk).reshape(bsz, seq, B_HEADS, B_DH).astype(f32) * (B_DH ** -0.5)
    v_b = bv.astype(f32).reshape(bsz, seq, B_HEADS, B_DH)
    i_pre = big.astype(f32) + b_ig.astype(f32)
    log_fg = jax.nn.log_sigmoid(bfg.astype(f32) + b_fg.astype(f32))
    h_b, c_new, n_new, m_new = mlstm_scan(q_b, k_b, v_b, i_pre, log_fg, c_m.astype(f32), n_m.astype(f32), m_m.astype(f32))
    h_b = jax.nn.sigmoid(bo.astype(f32)).reshape(bsz, seq, B_HEADS, B_DH) * layer_norm_heads(h_b, b_norm_g.reshape(B_HEADS, B_DH))
    y_b = h_b.reshape(bsz, seq, B_WIDTH).astype(x.dtype) @ w_pb
    merged = jax.nn.sigmoid(ga) * y_a + jax.nn.sigmoid(gb) * y_b
    out = merged @ w_o
    dt = x.dtype
    return out, (s_new.astype(dt), c_new.astype(dt), n_new.astype(dt), m_new.astype(dt), conv_new.astype(dt))

def swiglu(x, w_gate, w_up, w_down):
    return (jax.nn.silu(x @ w_gate) * (x @ w_up)) @ w_down

def moe_swiglu(x, w_router, b_router, w_gate, w_up, w_down):
    logits = (x @ w_router).astype(jnp.float32) + b_router.astype(jnp.float32)
    top_val, top_idx = lax.top_k(logits, TOP_K)
    top_w = jax.nn.softmax(top_val, axis=-1)
    gate = jnp.einsum('blk,blke->ble', top_w, jax.nn.one_hot(top_idx, N_EXPERTS, dtype=jnp.float32)).astype(x.dtype)
    out = jnp.zeros_like(x)
    for e in range(N_EXPERTS):
        out = out + gate[..., e:e + 1] * swiglu(x, w_gate[e], w_up[e], w_down[e])
    return out

def setup_inputs(seed: int = 0) -> dict:
    key = jax.random.key(seed)
    k = jax.random.split(key, 40)
    f32 = jnp.float32

    def nrm(i, shape, scale):
        return jax.random.normal(k[i], shape, f32) * scale

    part_scale = [D_MODEL ** -0.5] * len(IN_SIZES)
    part_scale[2] *= BETA
    part_scale[5] *= BETA
    col_scale = jnp.asarray(np.repeat(np.array(part_scale, np.float32), np.array(IN_SIZES)))
    return {
        'x_prompt': nrm(0, (BATCH, SEQ, D_MODEL), 1.0),
        'x_sample': nrm(1, (DEC_BATCH, DEC_SEQ, D_MODEL), 1.0),
        'state_hgrn': nrm(2, (DEPTH, DEC_BATCH, A_HEADS, A_DK, A_DV), 0.3),
        'state_mlstm_c': nrm(3, (DEPTH, DEC_BATCH, B_HEADS, B_DH, B_DH), 0.05),
        'state_mlstm_n': nrm(4, (DEPTH, DEC_BATCH, B_HEADS, B_DH), 0.1),
        'state_mlstm_m': jax.random.uniform(k[5], (DEPTH, DEC_BATCH, B_HEADS), f32, 0.0, 4.0),
        'state_conv': nrm(6, (DEPTH, DEC_BATCH, CONV_W - 1, B_WIDTH), 1.0),
        'w_in': nrm(7, (DEPTH, D_MODEL, N_IN), 1.0) * col_scale,
        'lb_param': nrm(8, (DEPTH, A_WIDTH_K), 0.5),
        'a_norm_g': 1.0 + nrm(9, (DEPTH, A_WIDTH_V), 0.02),
        'w_pa': nrm(10, (DEPTH, A_WIDTH_V, D_MODEL), A_WIDTH_V ** -0.5),
        'conv_w': nrm(11, (DEPTH, CONV_W, B_WIDTH), CONV_W ** -0.5),
        'conv_b': nrm(12, (DEPTH, B_WIDTH), 0.02),
        'w_q_blk': nrm(13, (DEPTH, N_QK_BLOCKS, QK_BLOCK, QK_BLOCK), QK_BLOCK ** -0.5),
        'w_k_blk': nrm(14, (DEPTH, N_QK_BLOCKS, QK_BLOCK, QK_BLOCK), QK_BLOCK ** -0.5),
        'b_ig': nrm(15, (DEPTH, B_HEADS), 0.1),
        'b_fg': jnp.linspace(3.0, 6.0, B_HEADS, dtype=f32)[None, :] + nrm(16, (DEPTH, B_HEADS), 0.1),
        'b_norm_g': 1.0 + nrm(17, (DEPTH, B_WIDTH), 0.02),
        'w_pb': nrm(18, (DEPTH, B_WIDTH, D_MODEL), B_WIDTH ** -0.5),
        'w_o': nrm(19, (DEPTH, D_MODEL, D_MODEL), BETA * D_MODEL ** -0.5),
        'ln1_g': 1.0 + nrm(20, (DEPTH, D_MODEL), 0.02),
        'ln1_b': nrm(21, (DEPTH, D_MODEL), 0.02),
        'ln2_g': 1.0 + nrm(22, (DEPTH, D_MODEL), 0.02),
        'ln2_b': nrm(23, (DEPTH, D_MODEL), 0.02),
        'w_ff_gate': nrm(24, (N_DENSE, D_MODEL, D_FF), D_MODEL ** -0.5),
        'w_ff_up': nrm(25, (N_DENSE, D_MODEL, D_FF), D_MODEL ** -0.5),
        'w_ff_down': nrm(26, (N_DENSE, D_FF, D_MODEL), BETA * D_FF ** -0.5),
        'w_router': nrm(27, (N_MOE, D_MODEL, N_EXPERTS), D_MODEL ** -0.5),
        'b_router': nrm(28, (N_MOE, N_EXPERTS), 0.01),
        'w_ex_gate': nrm(29, (N_MOE, N_EXPERTS, D_MODEL, D_FF), D_MODEL ** -0.5),
        'w_ex_up': nrm(30, (N_MOE, N_EXPERTS, D_MODEL, D_FF), D_MODEL ** -0.5),
        'w_ex_down': nrm(31, (N_MOE, N_EXPERTS, D_FF, D_MODEL), BETA * D_FF ** -0.5),
    }

def reference(x_prompt, x_sample, state_hgrn, state_mlstm_c, state_mlstm_n, state_mlstm_m, state_conv,
              w_in, lb_param, a_norm_g, w_pa, conv_w, conv_b, w_q_blk, w_k_blk, b_ig, b_fg, b_norm_g, w_pb, w_o,
              ln1_g, ln1_b, ln2_g, ln2_b, w_ff_gate, w_ff_up, w_ff_down,
              w_router, b_router, w_ex_gate, w_ex_up, w_ex_down):
    lb = jax.nn.softmax(lb_param.astype(jnp.float32), axis=0)
    lb = jnp.cumsum(lb, axis=0) - lb[:1]
    bp = x_prompt.shape[0]
    dt = x_prompt.dtype
    y_p, y_s = x_prompt, x_sample
    new_p = ([], [], [], [], [])
    new_s = ([], [], [], [], [])
    for l in range(DEPTH):
        mix_w = (w_in[l], lb[l], a_norm_g[l], w_pa[l], conv_w[l], conv_b[l], w_q_blk[l], w_k_blk[l],
                 b_ig[l], b_fg[l], b_norm_g[l], w_pb[l], w_o[l])
        zero_state = (jnp.zeros((bp, A_HEADS, A_DK, A_DV), dt), jnp.zeros((bp, B_HEADS, B_DH, B_DH), dt),
                      jnp.zeros((bp, B_HEADS, B_DH), dt), jnp.zeros((bp, B_HEADS), dt),
                      jnp.zeros((bp, CONV_W - 1, B_WIDTH), dt))
        past_state = (state_hgrn[l], state_mlstm_c[l], state_mlstm_n[l], state_mlstm_m[l], state_conv[l])
        outs = []
        for x, st, acc in ((y_p, zero_state, new_p), (y_s, past_state, new_s)):
            mixed, st_new = token_mixer(x, *st, *mix_w)
            x = layer_norm(ALPHA * x + mixed, ln1_g[l], ln1_b[l])
            j = l // 2
            if l % 2 == 0:
                ff = swiglu(x, w_ff_gate[j], w_ff_up[j], w_ff_down[j])
            else:
                ff = moe_swiglu(x, w_router[j], b_router[j], w_ex_gate[j], w_ex_up[j], w_ex_down[j])
            x = layer_norm(ALPHA * x + ff, ln2_g[l], ln2_b[l])
            for a, s in zip(acc, st_new):
                a.append(s)
            outs.append(x)
        y_p, y_s = outs
    hgrn_p, c_p, n_p, m_p, conv_p = (jnp.stack(a) for a in new_p)
    hgrn_s, c_s, n_s, m_s, conv_s = (jnp.stack(a) for a in new_s)
    return (y_p, y_s, hgrn_p, hgrn_s, c_p, c_s, n_p, n_s, m_p, m_s, conv_p, conv_s)


_drawn_inputs = setup_inputs


def setup_inputs(seed=0):
    import zlib

    import numpy as np

    out = dict(_drawn_inputs(seed))
    spreads = {}
    factors = {'a_norm_g': 8.0, 'b_norm_g': 16.741, 'b_router': 5.352}
    for name, (base, spread) in spreads.items():
        noise = np.random.default_rng([zlib.crc32(name.encode()), seed]).standard_normal(out[name].shape)
        drawn = base * np.exp(spread * noise) if base else spread * noise
        out[name] = __import__('jax').numpy.asarray(drawn.astype(out[name].dtype))
    for name, factor in factors.items():
        out[name] = (out[name] * factor).astype(out[name].dtype)
    return out
```

```python
from contextlib import ExitStack

import concourse.bass as bass
from concourse import mybir

P = 128
D = 1024
KC = D // P
SEQ = 256
DB, DS = 8, 8
NS = DB * DS
T = SEQ + NS
TT = [(0, 128), (128, 128), (256, 64)]
DEPTH = 2
HA = 8
HB = 4
CW = 4
UP = CW - 1
US = DS + UP
UW = UP + SEQ + DB * US
FF = 2816
FC = FF // P
NE = 8
NG = 256
EST = FF // NG
GATHER_AT = 8
SCATTER_AT = EST + 3
ALPHA = (2 * DEPTH) ** 0.25
EPS = 1e-5
TINY = 1e-30
NEG = -1e30
RING = 3
BLOCK = 128
SLOT = KC * 512

C_AQ, C_AF, C_AI, C_AG = 0, 1024, 2048, 3072
C_BU, C_BV, C_BO, C_BG = 4096, 5120, 6144, 7168
C_GA, C_GB = 7176, 8200

ALU = mybir.AluOpType
ACT = mybir.ActivationFunctionType
AX = mybir.AxisListType
F32 = mybir.dt.float32
F32R = mybir.dt.float32r
I32 = mybir.dt.int32
U8 = mybir.dt.uint8

PAR = {"lb": 0, "an": 2, "cw": 4, "cb": 12, "bn": 14, "g1": 16, "b1": 18, "g2": 20, "b2": 22}
NPAR = 24
LEVELS = 8


class Signals:

    def __init__(self, sem, table, tag):
        self.sem, self.table, self.tag, self.count = sem, table, tag, 0

    def done(self, *name):
        self.count += 1
        if name:
            self.table[(self.tag, *name)] = self.count
        return self.sem, 1

    def at(self, *name):
        key = (self.tag, *name)
        return self.sem, self.table[key] if "counted" in self.table else self.table.get(key, 1)

    def last(self):
        return self.sem, self.count


class Banks:

    def __init__(self, banks):
        self.banks, self.n, self.user = banks, 0, {}

    def take(self, name):
        b = self.banks[self.n % len(self.banks)]
        self.n += 1
        before = self.user.get(b)
        self.user[b] = name
        return b, before


def strips():
    out = []
    for hf in range(2):
        out += [("f", hf), ("q", hf), ("v", hf), ("g", hf)]
    out += [("bu", 0), ("bu", 1), ("bv", 0), ("bv", 1)]
    out += [("S", 0), ("S", 1)] + [("C", i) for i in range(4)]
    for name in ("pa", "ga", "bo", "gb", "pb", "wo"):
        out += [(name, 0), (name, 1)]
    return out


STRIPS = strips()
NSTRIP = len(STRIPS)
W_COL = {"f": C_AF, "q": C_AQ, "v": C_AI, "g": C_AG, "bu": C_BU, "bv": C_BV, "bo": C_BO, "ga": C_GA, "gb": C_GB}
MIX_OUT = {"pa": "w_pa", "pb": "w_pb", "wo": "w_o"}


def build(nc, I, O, table):
    ctx = ExitStack()
    with ctx:
        ctx.enter_context(nc.allow_non_contiguous_dma(reason="a few dozen words"))

        def sem(name):
            return ctx.enter_context(nc.semaphore(name))

        arena_floats = 40896
        arena = ctx.enter_context(nc.sbuf_tensor("arena", [P, arena_floats], F32))
        arena_at = nc.sbuf_base - 4 * arena_floats
        weights = ctx.enter_context(nc.sbuf_tensor("weights", [P, RING * SLOT], F32))
        cursor = [0]

        def rounded(name, at, *dims):
            n = 1
            for d in dims:
                n *= d
            v = nc.alloc_sbuf_tensor_at(name, [P, n], F32R, offset=arena_at + 4 * at)[:, :]
            if len(dims) == 2:
                v = v.rearrange("p (a b) -> p a b", a=dims[0])
            return v

        def place(n):
            a = cursor[0]
            cursor[0] += n
            return a

        def view(at, *dims, rows=P, dt=F32, of=None):
            n = 1
            for d in dims:
                n *= d
            v = (arena if of is None else of)[0:rows, at:at + n]
            if dt is not F32:
                v = v.bitcast(dt)
            if len(dims) == 2:
                v = v.rearrange("p (a b) -> p a b", a=dims[0])
            elif len(dims) == 3:
                v = v.rearrange("p (a b c) -> p a b c", a=dims[0], b=dims[1])
            elif len(dims) == 4:
                v = v.rearrange("p (a b c d) -> p a b c d", a=dims[0], b=dims[1], c=dims[2])
            return v

        xT = view(place(KC * T), KC, T)
        a_x1 = place(KC * T)
        x1T = view(a_x1, KC, T)
        ring = view(0, RING, SLOT, of=weights)
        par = view(place(KC * NPAR), KC, NPAR)
        lbc = view(place(DEPTH * 2 * KC), DEPTH, 2, KC)
        scT = view(place(KC * 48), KC, 48)
        ident = view(place(P), P)
        ones = view(place(P), P)
        causal = view(place(P), P)
        own8 = view(place(64), 64)
        levelm = view(place(7 * 32), 7 * 32).bitcast(U8).rearrange("p (l t) -> p l t", l=7)
        seg = view(place(DB), DB)
        blk4 = view(place(32), 32)
        sel = view(place(HB * P), HB, P, rows=HB)
        eps = view(place(1), 1)
        keep = view(place(T), T, rows=HB)
        drop = view(place(T), T, rows=HB)
        gbias = view(place(4), 4, rows=HB)
        m0r = view(place(2 * DB), 2, DB, rows=HB)
        n0T = view(place(64), 64)
        gw = view(place(KC * 8), KC, 8)
        wr = view(place(KC * NE), KC, NE)
        brt = view(place(NE), NE)
        rdS = view(place(HB * NS), HB, NS)
        colA = view(place(3 * 8), 3, 8)
        nP = view(place(8), 8)
        nS = view(place(64), 64)

        a_u = place(3072)
        a_x = place(10240)
        a_kt = place(3072)
        a_v = place(3072)
        a_att = place(2048)
        a_g = place(2560)
        a_o = place(2560)
        a_vb = place(3072)
        a_row = place(6 * T)
        a_st = place(T + NS + DB)
        H = 4 * T
        fP = [view(a_u, 4, T), view(a_x, 4, T)]
        qA = [view(a_u + H, 4, T), view(a_x + H, 4, T)]
        kA = view(a_x + 2 * H, 4, T)
        R = view(a_x + 3 * H, 4, T)
        Qe = [view(a_x + 4 * H, 4, T), view(a_x + 5 * H, 4, T)]
        Ke = [view(a_x + 6 * H, 4, T), view(a_x + 7 * H, 4, T)]
        kTok = view(a_kt, 3, D)
        vTok = view(a_v, 3, D)
        attD = view(a_att, 2, 4, P)
        attX = view(a_att + 1024, 4, P)
        attS = view(a_att + 1536, HA, NS, rows=NS)
        gS = view(a_g, KC, T)
        oA = view(a_o, KC, T)
        stP = view(a_x1 + 2 * D, 4, P)
        qS = view(place(HA * NS), HA, NS)
        decA = view(place(HA * DB), HA, DB)
        kmA = [view(a_x1 + i * D, D) for i in range(2)]
        sqA = view(a_x1, KC, T)
        eb = [view(a_x1 + i * (T + NS + DB), T + NS + DB) for i in range(2)]
        rsA = view(a_x + 4 * H, KC, T)
        U = view(a_u, KC, UW)
        uS = view(a_x + 4 * H, KC, T)
        qB = view(a_x, KC, T)
        kB = view(a_x + 2 * H, KC, T)
        hB = view(a_x + 6 * H, KC, T)
        vB = view(a_vb, 3, D)
        kTB = view(a_u, 3, D)
        bdq = view(a_kt, KC, P)
        bdk = view(a_kt + 1024, KC, P)
        qI = view(a_kt + 2048, HA, NS)
        qn = view(a_kt + 2560, HA, NS)
        qz = [view(a_kt + i * HA * NS, HA, NS) for i in range(2)]
        interS = view(a_kt + 2 * HA * NS, 2, 512, rows=NS)
        wW = [view(a_att + i * 448, 448) for i in range(2)]
        sW = [view(a_att + 896 + i * 448, 448) for i in range(2)]
        kmB = [view(a_x1 + i * D, D) for i in range(2)]
        cvg = view(a_v, KC, 27)
        cvo = view(a_v + 256, D, rows=27)
        wq4 = view(place(KC * 4), KC, 4)
        wk4 = view(place(KC * 4), KC, 4)
        rd = [view(a_v + 1408 + i * T, T) for i in range(2)]
        cP = view(a_v + 2048, 2, 256)
        nrow = view(a_v + 2560, P, rows=64)
        nrowP = view(a_v + 2688, P, rows=8)
        tg = [view(a_att + i * T, T) for i in range(2)]
        decB = view(place(HB * DB), HB, DB)
        mout = view(place(DB + 1), DB + 1, rows=HB)
        rows = [view(a_row + i * T, T, rows=HB) for i in range(6)]
        bcr = view(a_st, T + NS + DB, rows=HB)
        sqB = view(a_x1, KC, T)
        rsB = view(a_x, KC, T)
        boS = view(a_x + 2 * H, KC, T)
        gbS = view(a_x + 4 * H, KC, T)
        yA = view(a_g, KC, T)
        merged = view(a_o, KC, T)
        sqL = view(a_x, KC, T)
        rstd = view(a_x + 2880, T)
        hT = view(a_x, FC, T)
        silu = [view(a_x + FC * T + i * T, T) for i in range(2)]

        def aligned(a):
            return -(-a // 8) * 8

        w1h = [rounded("w1_high0", 0, KC, 512), rounded("w1_high1", aligned(a_u), KC, 512)]
        w1l = [rounded("w1_rest0", aligned(a_v), KC, 512), rounded("w1_rest1", aligned(a_o), KC, 512)]
        w2h = rounded("w2_high", aligned(a_o) + SLOT, 2, D)
        w2l = rounded("w2_rest", aligned(a_o) + SLOT + 2 * D, 2, D)
        def down_split(q):
            if q < 2 * EST - 2:
                return w2h, w2l
            k = slice(0, 4) if q == 2 * EST - 2 else slice(4, 8)
            return [w[0][:, k].rearrange("p (f i) n -> p f (i n)", f=2) for w in (w1h, w1l)]

        at = [aligned(a_u) + SLOT]

        def room(*dims, rows=P, dt=F32):
            n = 1
            for d in dims:
                n *= d
            at[0] += n
            assert at[0] <= a_x + 10240
            return view(at[0] - n, *dims, rows=rows, dt=dt)

        def rounded_room(name, *dims):
            at[0] = aligned(at[0]) + dims[0] * dims[1]
            assert at[0] <= a_x + 10240
            return rounded(name, at[0] - dims[0] * dims[1], *dims)

        xtk = view(a_kt, 3, D)
        acc = view(a_g, KC, T)
        xgh = [rounded_room(f"tokens_high{i}", KC, BLOCK) for i in range(2)]
        xgl = [rounded("tokens_rest0", SLOT, KC, BLOCK), rounded_room("tokens_rest1", KC, BLOCK)]
        hidh = [rounded_room(f"hidden_high{i}", 2, P) for i in range(2)]
        hidl = [rounded("hidden_rest0", aligned(a_v) + SLOT, 2, P), rounded("hidden_rest1", aligned(a_v) + SLOT + 2 * P, 2, P)]
        selm = [room(3, BLOCK) for _ in range(2)]
        gsel = [room(3, BLOCK) for _ in range(2)]
        gselT = [room(T) for _ in range(2)]
        sil = [room(NG) for _ in range(2)]
        hid = [room(NG) for _ in range(2)]
        ysb = room(D)
        lg, expl, chosen, gate, pos = [room(3, NE) for _ in range(5)]
        cmp1, cmp2 = [room(3, NE, NE) for _ in range(2)]
        mx3 = room(3)
        after_ = room(P)
        iotaI = room(P, dt=I32)
        iotaF = room(P)
        tri8 = room(NE, NE)
        cnt = room(1)
        over_all = room(1, dt=I32)
        over = over_all[0:1, 0:1]
        mo_w1 = [view(i * SLOT, KC, 512, of=weights) for i in range(2)]
        mo_w2 = [view(2 * SLOT + i * 2 * D, 2, D, of=weights) for i in range(2)]
        ff_w1 = [view(i * 2 * D, 2, KC, P, of=weights) for i in range(2)]
        ff_w2 = [view(SLOT + i * FC * P, FC, P, of=weights) for i in range(2)]
        e_x = view(a_v, 3, D)
        e_par = view(a_u, D, rows=NPAR)
        e_conv = view(a_u + D, D, rows=48)
        n0row = view(a_o, P, rows=64)
        rowI = view(a_g, P, dt=I32)
        colI = view(a_g + P, P, dt=I32)
        xorI = view(a_g + 2 * P, P, dt=I32)
        xorF = view(a_g + 3 * P, P)
        maskt = view(a_g + 4 * P, P)
        row3 = view(a_g + 5 * P, 1, dt=I32)
        row2 = view(a_g + 5 * P + 1, 1, dt=I32)
        laterT = view(a_g + 6 * P, P)
        lbt = view(place(KC), KC)
        yrow = view(a_v, 3, D)

        assert cursor[0] <= arena_floats, cursor[0]
        bank = [ctx.enter_context(nc.psum_tensor(f"bank{i}", [P, 512], F32))[:, :] for i in range(8)]

        pe_s = Signals(sem("tensor_steps"), table, "pe")
        ac_s = Signals(sem("scalar_steps"), table, "act")
        dv_s = Signals(sem("vector_steps"), table, "dve")
        po_s = Signals(sem("pool_steps"), table, "pool")
        ring_full = [sem(f"ring_full{i}") for i in range(RING)]
        load = {n: sem(f"load_{n}") for n in ("x", "par", "conv", "gates", "bias", "w4", "n0", "router")}
        stored = {n: sem(f"stored_{n}") for n in ("S0", "S1", "C0", "C1", "C2", "C3", "st", "cp", "conv", "n", "m", "y", "y2")}
        ff_in, ff_in2, ff_gate, ff_up, ff_silu, ff_h, ff_down, ff_res = [
            [sem(f"ff_{n}{s}") for s in range(2)]
            for n in ("columns_landed", "down_landed", "gate_done", "up_done", "silu_done", "hidden_done", "down_done",
                      "residual_done")]
        moe_in, moe_in2, mo_w1h, mo_w1l, mo_w2h, mo_w2l, mo_sel, mo_gsel, mo_gath, mo_gu, mo_sil, mo_h, mo_turn, mo_hh, mo_hl, mo_down = [
            [sem(f"moe_{n}{s}") for s in range(2)]
            for n in ("columns_landed", "down_landed", "columns_high", "columns_rest", "down_high", "down_rest",
                      "selection_made", "gates_selected", "gathered", "gate_up_done", "silu_done", "hidden_done", "hidden_turned",
                      "hidden_high", "hidden_rest", "down_done")]
        mo_xh, mo_xg, mo_ys, mo_sc, mo_acc, mo_shift, mo_a, mo_v = [
            sem(f"moe_{n}") for n in ("tokens_high", "tokens_in_sbuf", "outputs_in_sbuf", "scattered", "added", "shifted",
                                      "scalar_steps", "vector_steps")]
        ENG = {"pe": pe_s, "act": ac_s, "dve": dv_s, "pool": po_s}

        pools = {"G": Banks([0, 1]), "L": Banks([2, 3, 4]), "M": Banks([5, 6]), "S": Banks([7])}
        uses = {}

        def claim(pe, pool, *name):
            b, before = pools[pool].take(name)
            uses[name] = b
            table[("bank", *name)] = b
            if before is not None:
                tag = table.get(("freed", *before))
                if tag is not None:
                    pe.wait_ge(*ENG[tag].at("free", *before))
            return bank[b]

        def of(*name):
            return bank[table.get(("bank", *name), 0)]

        def free(sig, *name):
            table[("freed", *name)] = sig.tag
            return sig.done("free", *name)

        def blocks(t, h, n):
            if n == T:
                return t.rearrange("p g t -> p (g t)").rearrange("p (n two h) -> p n two h", two=2, h=h)
            return t[:, :, 0:n].rearrange("p g (n two h) -> p g n two h", two=2, h=h)

        def half(v, side, h, last=False):
            w = slice(h - 1, h) if last else slice(0, h)
            return v[:, :, side, w] if len(v.shape) == 4 else v[:, :, :, side, w]

        def strip_at(l, name, i):
            n = l * NSTRIP + STRIPS.index((name, i))
            return ring[:, n % RING, :], ring_full[n % RING], 16 * (n // RING + 1)

        block = ctx.enter_context(nc.Block())
        def chunk(n):
            return slice(n * P, (n + 1) * P)

        @block.tensor
        def _(pe):
            for s in ff_up + ff_down + mo_gu + mo_down + mo_gath:
                pe.sem_inc(s, 1)

            def project(l, name, i, m, src, freed=False):
                w, full, n = strip_at(l, name, i)
                w = w.rearrange("p (k n) -> p k n", k=KC)
                if m == 0:
                    pe.wait_ge(full, n)
                out = claim(pe, "G", l, name, i, m)
                for k in range(KC):
                    mm = nc.tensor.matmul(out[:, 0:T], w[:, k, chunk(m)], src[:, k, :], start=k == 0, stop=k == KC - 1)
                mm.then_inc(*pe_s.done("mm", l, name, i, m))
                if m == 3:
                    table[("pe", "strip", l, name, i)] = pe_s.count

            def project_rows(l, name, i, t):
                w, full, n = strip_at(l, name, i)
                w = w.rearrange("p (k n) -> p k n", k=KC)
                if t == 0:
                    pe.wait_ge(full, n)
                out = claim(pe, "G", l, name, i, t)
                t0, r = TT[t]
                for k in range(KC):
                    mm = nc.tensor.matmul(out[0:r, :], xT[:, k, t0:t0 + r], w[:, k, :], start=k == 0, stop=k == KC - 1)
                mm.then_inc(*pe_s.done("mm", l, name, i, t))
                if t == 2:
                    table[("pe", "strip", l, name, i)] = pe_s.count

            def level(l, hf, lv):
                if lv < 0:
                    a, b = kA, qA[hf]
                    pe.wait_ge(*dv_s.at("prep", l, hf))
                    pe.wait_ge(*ac_s.at("silu q", l, hf))
                else:
                    a, b = Ke[lv % 2], Qe[lv % 2]
                    pe.wait_ge(*dv_s.at("operands", l, hf, lv))
                if lv == 7:
                    out = claim(pe, "L", l, "level", hf, lv, 0)
                    for j in range(4):
                        mm = nc.tensor.matmul(out[:, chunk(j)], a[:, j, 0:128], b[:, j, 128:256], start=True, stop=True)
                    mm.then_inc(*pe_s.done("level", l, hf, lv, 0))
                    return
                for t in range(3 if lv <= 2 else 2):
                    t0, r = TT[t]
                    out = claim(pe, "L", l, "level", hf, lv, t)
                    for j in range(4):
                        mm = nc.tensor.matmul(out[0:r, j * r:(j + 1) * r], a[:, j, t0:t0 + r], b[:, j, t0:t0 + r],
                                              start=True, stop=True)
                    mm.then_inc(*pe_s.done("level", l, hf, lv, t))

            def key_rows(l, hf):
                pe.wait_ge(*dv_s.at("key end", l, hf))
                for t, (t0, r) in enumerate(TT):
                    out = claim(pe, "M", l, "kt", hf, t)
                    for j in range(4):
                        mm = nc.tensor.transpose(out[0:r, chunk(j)], Ke[0][:, j, t0:t0 + r], ident)
                    mm.then_inc(*pe_s.done("kt", l, hf, t))

            def prompt_heads(l, hf):
                pe.wait_ge(*dv_s.at("att", l, hf))
                pe.wait_ge(*ac_s.at("cross", l, hf))
                pe.wait_ge(*ac_s.at("v", l, "v", hf, 2))
                out = claim(pe, "L", l, "o", hf, 0)
                for j in range(4):
                    mm = nc.tensor.matmul(out[:, chunk(j)], vTok[:, 0, chunk(4 * hf + j)], attD[:, 0, j, :],
                                          start=True, stop=True)
                mm.then_inc(*pe_s.done("o", l, hf, 0))
                out = claim(pe, "L", l, "o", hf, 1)
                for j in range(4):
                    nc.tensor.matmul(out[:, chunk(j)], vTok[:, 0, chunk(4 * hf + j)], attX[:, j, :],
                                     start=True, stop=False)
                    mm = nc.tensor.matmul(out[:, chunk(j)], vTok[:, 1, chunk(4 * hf + j)], attD[:, 1, j, :],
                                          start=False, stop=True)
                mm.then_inc(*pe_s.done("o", l, hf, 1))
                pe.wait_ge(*ac_s.at("kt", l, hf, 2))
                out = claim(pe, "M", l, "st", hf)
                for j in range(4):
                    h = 4 * hf + j
                    nc.tensor.matmul(out[:, chunk(j)], kTok[:, 0, chunk(h)], vTok[:, 0, chunk(h)], start=True, stop=False)
                    mm = nc.tensor.matmul(out[:, chunk(j)], kTok[:, 1, chunk(h)], vTok[:, 1, chunk(h)],
                                          start=False, stop=True)
                mm.then_inc(*pe_s.done("st", l, hf))

            def sampled_hgrn(l):
                out = claim(pe, "S", l, "oS")
                oS = out.rearrange("p (h t) -> p h t", h=HA)
                for h in range(HA):
                    nc.tensor.matmul(oS[:, h, :], vTok[0:NS, 2, chunk(h)], attS[:, h, :], start=h == 0, stop=False,
                                     skip_group_check=True)
                pe.wait_ge(*dv_s.at("qS", l, 1))
                pe.wait_ge(*dv_s.at("rows padded", l))
                for b in range(DB):
                    if b % 4 == 0:
                        w, full, n = strip_at(l, "S", b // 4)
                        pe.wait_ge(full, n)
                        s0 = w.rearrange("p (b h v) -> p b h v", b=4, h=HA)
                    for h in range(HA):
                        mm = nc.tensor.matmul(oS[:, h, b * DS:(b + 1) * DS], s0[:, b % 4, h, :],
                                              qS[:, h, b * DS:(b + 1) * DS], start=False, stop=b == DB - 1,
                                              skip_group_check=True)
                    mm.then_inc(*pe_s.done("inter", l, b))
                    pe.wait_ge(*po_s.at("kmA", l, b))
                    for q in range(2):
                        out = claim(pe, "M", l, "dS", b, q)
                        for j in range(4):
                            h = 4 * q + j
                            mm = nc.tensor.matmul(out[:, chunk(j)], kmA[b % 2][:, chunk(h)], vTok[:, 2, chunk(h)],
                                                  start=True, stop=True)
                        mm.then_inc(*pe_s.done("dS", l, b, q))

            def head_sums(l, name, src, n, each, sig, *ready):
                pe.wait_ge(*sig.at(*ready))
                for h in range(n):
                    out = claim(pe, "M", l, name, h)
                    for c in range(each):
                        mm = nc.tensor.matmul(out[:, 0:T], ones, src[:, each * h + c, :], start=c == 0, stop=c == each - 1)
                    mm.then_inc(*pe_s.done(name, l, h))

            def gates(l):
                pe.wait_ge(load["gates"], 16 * (l + 1))
                for g in range(2):
                    out = claim(pe, "G", l, "gate", g)
                    for k in range(KC):
                        mm = nc.tensor.matmul(out[0:HB, 0:T], gw[:, k, 4 * g:4 * g + 4], xT[:, k, :],
                                              start=k == 0, stop=k == KC - 1)
                    mm.then_inc(*pe_s.done("gate", l, g))

            def conv_rows(l):
                pe.wait_ge(*dv_s.at("cvg", l))
                for i in range(2):
                    out = claim(pe, "M", l, "cv", i)
                    for c in range(4):
                        mm = nc.tensor.transpose(out[0:27, chunk(c)], cvg[:, 4 * i + c, :], ident)
                    mm.then_inc(*pe_s.done("cv", l, i))

            def qk_blocks(l):
                pe.wait_ge(*dv_s.at("bd", l))
                pe.wait_ge(*ac_s.at("silu u", l))
                for c in range(KC):
                    for name, w in (("qB", bdq), ("kB", bdk)):
                        out = claim(pe, "G", l, name, c)
                        nc.tensor.matmul(out[:, 0:T], w[:, c, :], uS[:, c, :], start=True, stop=True)\
                            .then_inc(*pe_s.done(name, l, c))

            def gate_columns(l):
                pe.wait_ge(*ac_s.at("wst", l))
                out = claim(pe, "M", l, "col")
                for t, (t0, r) in enumerate(TT):
                    nc.tensor.transpose(out[0:r, 8 * t:8 * t + 4], rows[2][:, t0:t0 + r], ident[0:HB, 0:HB])
                    mm = nc.tensor.transpose(out[0:r, 8 * t + 4:8 * t + 8], rows[5][:, t0:t0 + r], ident[0:HB, 0:HB])
                mm.then_inc(*pe_s.done("col", l))

            def mlstm_spread(l, h):
                pe.wait_ge(*ac_s.at("bcr", l))
                out = claim(pe, "M", l, "spread", h, 0)
                nc.tensor.matmul(out[:, 0:T], sel[:, h, :], rows[3], start=True, stop=True)\
                    .then_inc(*pe_s.done("spread", l, h, 0))
                out = claim(pe, "M", l, "spread", h, 1)
                nc.tensor.matmul(out[:, 0:T + NS + DB], sel[:, h, :], bcr, start=True, stop=True)\
                    .then_inc(*pe_s.done("spread", l, h, 1))

            def mlstm_scores(l, h):
                pe.wait_ge(*ac_s.at("qkB", l, 2 * h + 1))
                out = claim(pe, "L", l, "s", h)
                for s0, r, t0, n, o in ((0, 128, 0, 256, 0), (128, 128, 128, 128, 256), (256, 64, 256, 64, 384)):
                    for c in range(2):
                        mm = nc.tensor.matmul(out[0:r, o:o + n], kB[:, 2 * h + c, s0:s0 + r],
                                              qB[:, 2 * h + c, t0:t0 + n], start=c == 0, stop=c == 1)
                mm.then_inc(*pe_s.done("s", l, h))

            def mlstm_keys(l, h):
                for t, (t0, r) in enumerate(TT):
                    out = claim(pe, "M", l, "ktB", h, t)
                    for c in range(2):
                        mm = nc.tensor.transpose(out[0:r, chunk(c)], kB[:, 2 * h + c, t0:t0 + r], ident)
                    mm.then_inc(*pe_s.done("ktB", l, h, t))

            def mlstm_values(l, h):
                s = sW[h % 2]
                pe.wait_ge(*dv_s.at("sw", l, h))
                pe.wait_ge(*dv_s.at("qn", l, h))
                pe.wait_ge(*ac_s.at("v", l, "bv", 1, 2))
                out = claim(pe, "L", l, "num", h)
                for c in range(2):
                    v = slice(h * 256 + c * P, h * 256 + (c + 1) * P)
                    o = 256 * c
                    nc.tensor.matmul(out[:, o:o + 128], vB[:, 0, v], s[:, 0:128], start=True, stop=True)
                    nc.tensor.matmul(out[:, o + 128:o + 256], vB[:, 0, v], s[:, 128:256], start=True, stop=False)
                    mm = nc.tensor.matmul(out[:, o + 128:o + 256], vB[:, 1, v], s[:, 256:384], start=False, stop=True)
                mm.then_inc(*pe_s.done("num", l, h))
                out = claim(pe, "L", l, "den", h)
                nc.tensor.matmul(out[:, 0:128], ones, s[:, 0:128], start=True, stop=True)
                nc.tensor.matmul(out[:, 128:256], ones, s[:, 128:256], start=True, stop=False)
                nc.tensor.matmul(out[:, 128:256], ones, s[:, 256:384], start=False, stop=True)
                nc.tensor.matmul(out[:, 256:320], ones[0:NS, :], s[0:NS, 384:448], start=True, stop=False)
                for c in range(2):
                    mm = nc.tensor.matmul(out[:, 256:320], ones, qn[:, 2 * h + c, :], start=False, stop=c == 1)
                mm.then_inc(*pe_s.done("den", l, h))
                if h == 0:
                    claim(pe, "S", l, "nS")
                nu = of(l, "nS").rearrange("p (h t) -> p h t", h=HA)
                for c in range(2):
                    v = slice(h * 256 + c * P, h * 256 + (c + 1) * P)
                    mm = nc.tensor.matmul(nu[:, 2 * h + c, :], vB[0:NS, 2, v], s[0:NS, 384:448],
                                          start=h == 0 and c == 0, stop=False, skip_group_check=True)
                mm.then_inc(*pe_s.done("intra", l, h))
                pe.wait_ge(*dv_s.at("ktB", l, h, 2))
                out = claim(pe, "M", l, "cP", h)
                for c in range(2):
                    kc = slice(h * 256 + c * P, h * 256 + (c + 1) * P)
                    for t in range(2):
                        mm = nc.tensor.matmul(out[:, c * 256:(c + 1) * 256], kTB[:, t, kc],
                                              vB[:, t, h * 256:(h + 1) * 256], start=t == 0, stop=t == 1)
                mm.then_inc(*pe_s.done("cP", l, h))
                out = claim(pe, "M", l, "nn", h)
                for c in range(2):
                    kc = slice(h * 256 + c * P, h * 256 + (c + 1) * P)
                    for t in range(2):
                        nc.tensor.matmul(out[:, 16 + c:17 + c], kTB[:, t, kc], ones[:, 0:1], start=t == 0, stop=t == 1)
                    mm = nc.tensor.matmul(out[:, 8 * c:8 * c + 8], kTB[0:NS, 2, kc], seg[0:NS, :], start=True, stop=True)
                mm.then_inc(*pe_s.done("nn", l, h))

            def sampled_mlstm(l):
                inter = [claim(pe, "L", l, "interB", i) for i in range(2)]
                for b in range(DB):
                    if b % 2 == 0:
                        w, full, n = strip_at(l, "C", b // 2)
                        pe.wait_ge(full, n)
                        c0 = w.rearrange("p (b h c v) -> p b h c v", b=2, h=HB, c=2)
                    pe.wait_ge(*po_s.at("qz", l, b))
                    for h in range(HB):
                        o = 256 * (h % 2)
                        for c in range(2):
                            mm = nc.tensor.matmul(inter[h // 2][0:NS, o:o + 256], qz[b % 2][:, 2 * h + c, :],
                                                  c0[:, b % 2, h, c, :], start=b == 0 and h % 2 == 0 and c == 0,
                                                  stop=b == DB - 1, skip_group_check=True)
                    mm.then_inc(*pe_s.done("interB", l, b))
                    pe.wait_ge(*po_s.at("kmB", l, b))
                    for h in range(HB):
                        out = claim(pe, "M", l, "dC", b, h)
                        for c in range(2):
                            kc = slice(h * 256 + c * P, h * 256 + (c + 1) * P)
                            mm = nc.tensor.matmul(out[:, c * 256:(c + 1) * 256], kmB[b % 2][:, kc],
                                                  vB[:, 2, h * 256:(h + 1) * 256], start=True, stop=True)
                        mm.then_inc(*pe_s.done("dC", l, b, h))

            def inter_turned(l):
                nu = of(l, "nS").rearrange("p (h t) -> p h t", h=HA)
                for i in range(2):
                    pe.wait_ge(*ac_s.at("free", l, "interB", i))
                    for c in range(4):
                        mm = nc.tensor.matmul(nu[:, 4 * i + c, :], interS[:, i, chunk(c)], ident[0:NS, 0:NS],
                                              start=False, stop=True, skip_group_check=True)
                mm.then_inc(*pe_s.done("nS", l))

            def normaliser_rows(l):
                pe.wait_ge(*dv_s.at("nS", l, HB - 1))
                out = claim(pe, "M", l, "nrow")
                nc.tensor.transpose(out[0:64, 0:P], nS, ident)
                nc.tensor.transpose(out[0:8, P:2 * P], nP, ident).then_inc(*pe_s.done("nrow", l))

            def width_sums(l, name, src, sig=None, step=None):
                out = claim(pe, "M", l, name)
                for k in range(KC):
                    if sig is not None:
                        pe.wait_ge(*sig.at(step, l, k))
                    mm = nc.tensor.matmul(out[:, 0:T], ones, src[:, k, :], start=k == 0, stop=k == KC - 1)
                mm.then_inc(*pe_s.done(name, l))

            def to_rows(l, name, src, sig, *ready):
                pe.wait_ge(*sig.at(*ready))
                for t, (t0, r) in enumerate(TT):
                    for i in range(2):
                        out = claim(pe, "M", l, name, t, i)
                        for c in range(4):
                            mm = nc.tensor.transpose(out[0:r, chunk(c)], src[:, 4 * i + c, t0:t0 + r], ident)
                        mm.then_inc(*pe_s.done(name, l, t, i))

            def experts(it0):
                def split_product(out, xh, xl, wh, wl, start, stop):
                    nc.tensor.matmul(out, xh, wh, start=start, stop=False)
                    nc.tensor.matmul(out, xh, wl, start=False, stop=False)
                    return nc.tensor.matmul(out, xl, wh, start=False, stop=stop)

                with pe.Fori(0, NE // 2) as pr:
                    it = it0 + pr

                    def gather(ei):
                        pe.wait_ge(mo_sel[ei], it + 1)
                        pe.wait_ge(mo_acc, 16 * it + 1)
                        for k in range(KC):
                            for t, (t0, r) in enumerate(TT):
                                nc.tensor.matmul(bank[5 + k // 4][:, chunk(k % 4)], xtk[:, t, chunk(k)],
                                                 selm[ei][:, t, :], start=t == 0, stop=t == 2)
                        pe.wait_ge(mo_gsel[ei], it + 1)
                        for t, (t0, r) in enumerate(TT):
                            mm = nc.tensor.transpose(bank[7][:, t0:t0 + r], gsel[ei][0:r, t, :], ident[0:r, 0:r])
                        mm.then_inc(mo_gath[ei], 1)

                    def gate_up(q):
                        s, ei = q % 2, q // EST
                        if q % EST == 0:
                            pe.wait_ge(mo_xg, 2 * it + ei + 1)
                        pe.wait_ge(mo_w1l[s], it * EST + q // 2 + 2)
                        pe.wait_ge(mo_h[s], it * EST + q // 2 + 1)
                        for k in range(KC):
                            mm = split_product(bank[s], xgh[ei][:, k, :], xgl[ei][:, k, :], w1h[s][:, k], w1l[s][:, k],
                                               k == 0, k == KC - 1)
                        mm.then_inc(mo_gu[s], 1)

                    def turn(q):
                        pe.wait_ge(mo_h[q % 2], it * EST + q // 2 + 2)
                        pe.wait_ge(mo_hl[(q + 1) % 2], it * EST + (q + 1) // 2 + 1)
                        for f in range(2):
                            mm = nc.tensor.transpose(bank[2][:, 256 * (q % 2) + f * P:256 * (q % 2) + (f + 1) * P],
                                                     hid[q % 2][:, chunk(f)], ident)
                        mm.then_inc(mo_turn[q % 2], 1)

                    def down(q):
                        j = q % EST
                        if q == EST:
                            pe.wait_ge(mo_ys, 2 * it + 1)
                        pe.wait_ge(mo_hl[q % 2], it * EST + q // 2 + 2)
                        pe.wait_ge(mo_w2l[q % 2], it * EST + q // 2 + 2)
                        for f in range(2):
                            for i in range(2):
                                n = slice(512 * i, 512 * i + 512)
                                high, rest = down_split(q)
                                mm = split_product(bank[3 + i], hidh[q % 2][:, f, :], hidl[q % 2][:, f, :],
                                                   high[:, f, n], rest[:, f, n],
                                                   j == 0 and f == 0, j == EST - 1 and f == 1)
                        mm.then_inc(mo_down[q % 2], 1)

                    def scatter(ei):
                        x = 2 * it + ei
                        pe.wait_ge(mo_ys, x + 1)
                        if ei == 0:
                            pe.wait_ge(mo_xg, x + 2)
                        else:
                            pe.wait_ge(mo_acc, 8 * x + 1)
                        for c in range(KC):
                            if c >= 3:
                                pe.wait_ge(mo_acc, 8 * x + c - 1)
                            nc.tensor.matmul(bank[(7, 5, 6)[c % 3]][:, 0:T], ysb[:, chunk(c)], gselT[ei],
                                             start=True, stop=True).then_inc(mo_sc, 1)

                    gather(0)
                    for q in range(2 * EST + 2):
                        if q < 2 * EST:
                            gate_up(q)
                        if 1 <= q <= 2 * EST:
                            turn(q - 1)
                        if q >= 2:
                            down(q - 2)
                        if q == GATHER_AT:
                            gather(1)
                        if q == SCATTER_AT:
                            scatter(0)
                    scatter(1)

            def tensor_moe(l):
                to_rows(l, "xt", x1T, ac_s, "ln1", l, KC - 1)
                pe.wait_ge(load["router"], 32)
                out = claim(pe, "M", l, "logits")
                for t, (t0, r) in enumerate(TT):
                    for k in range(KC):
                        mm = nc.tensor.matmul(out[0:r, NE * t:NE * t + NE], x1T[:, k, t0:t0 + r], wr[:, k, :],
                                              start=k == 0, stop=k == KC - 1)
                mm.then_inc(*pe_s.done("logits"))
                pe.wait_ge(*dv_s.at("chosen"))
                out = claim(pe, "M", l, "ranks")
                for t, (t0, r) in enumerate(TT):
                    for u in range(t + 1):
                        ru = TT[u][1]
                        mm = nc.tensor.matmul(out[0:r, NE * t:NE * t + NE], (ones if u < t else after_)[0:ru, 0:r],
                                              chosen[0:ru, u, :], start=u == 0, stop=u == t)
                for u, (_, ru) in enumerate(TT):
                    mm = nc.tensor.matmul(out[:, 24:32], ones[0:ru, :], chosen[0:ru, u, :], start=u == 0, stop=u == 2)
                mm.then_inc(*pe_s.done("ranks"))
                pe.wait_ge(*dv_s.at("pos"))
                pe.wait_ge(*ac_s.at("xtk"))
                experts(0)
                flag = pe.value_load(over, min_val=0, max_val=1)
                with pe.If(flag > 0):
                    with pe.Fori(1, 3) as ps:
                        experts(ps * (NE // 2))
                    pe.wait_ge(mo_acc, 3 * NE * KC + 1)
                pe.wait_ge(mo_acc, NE * KC + 1)

            pe.wait_ge(*po_s.at("ident"))
            pe.wait_ge(load["x"], 32)
            for t, (t0, r) in enumerate(TT):
                for i in range(2):
                    out = claim(pe, "M", 0, "xin", t, i)
                    for c in range(4):
                        mm = nc.tensor.transpose(out[:, c * P:c * P + r], e_x[0:r, t, chunk(4 * i + c)], ident[0:r, 0:r])
                    mm.then_inc(*pe_s.done("xin", t, i))
            pe.wait_ge(load["par"], 16 * 9)
            out = claim(pe, "M", 0, "par")
            for c in range(KC):
                mm = nc.tensor.transpose(out[:, c * NPAR:(c + 1) * NPAR], e_par[:, chunk(c)], ident[0:NPAR, 0:NPAR])
            mm.then_inc(*pe_s.done("par"))
            pe.wait_ge(load["conv"], 16)
            out = claim(pe, "M", 0, "scT")
            for c in range(KC):
                mm = nc.tensor.transpose(out[:, c * 48:(c + 1) * 48], e_conv[:, chunk(c)], ident[0:48, 0:48])
            mm.then_inc(*pe_s.done("scT"))

            for l in range(DEPTH):
                pe.wait_ge(load["n0"], 16 * (l + 1))
                out = claim(pe, "M", l, "n0")
                nc.tensor.transpose(out[:, 0:64], n0row, ident[0:64, 0:64]).then_inc(*pe_s.done("n0", l))
                if l == 0:
                    pe.wait_ge(*ac_s.at("xT", 0))
                else:
                    pe.wait_ge(*ac_s.at("ln2", 0, KC - 1))
                for name in ("f", "q"):
                    for m in range(4):
                        project(l, name, 0, m, xT)
                tiles = {0: [("v", 0, t) for t in range(3)] + [(n, i, m) for n, i in (("g", 0), ("f", 1), ("q", 1)) for m in range(4)],
                         1: [("v", 1, t) for t in range(3)] + [(n, i, m) for n, i in (("g", 1), ("bu", 0), ("bu", 1)) for m in range(4)]
                         + [("bv", i, t) for i in range(2) for t in range(3)]}
                for hf in range(2):
                    todo = list(tiles[hf])

                    def step():
                        if todo:
                            name, i, m = todo.pop(0)
                            if name in ("v", "bv"):
                                project_rows(l, name, i, m)
                            else:
                                project(l, name, i, m, xT)

                    step()
                    step()
                    for lv in range(-1, LEVELS):
                        level(l, hf, lv)
                        step()
                    key_rows(l, hf)
                    step()
                    prompt_heads(l, hf)
                    while todo:
                        step()
                gates(l)
                sampled_hgrn(l)
                conv_rows(l)
                qk_blocks(l)
                gate_columns(l)
                for h in range(HB):
                    mlstm_spread(l, h)
                    mlstm_scores(l, h)
                    mlstm_keys(l, h)
                    mlstm_values(l, h)
                head_sums(l, "rms", sqA, HA, 1, ac_s, "sqA", l)
                sampled_mlstm(l)
                inter_turned(l)
                normaliser_rows(l)
                def project_all(name, src):
                    for i in range(2):
                        for m in range(4):
                            project(l, name, i, m, src)

                pe.wait_ge(*dv_s.at("oA", l))
                project_all("pa", oA)
                head_sums(l, "muB", hB, HB, 2, dv_s, "hB", l)
                project_all("ga", xT)
                head_sums(l, "varB", sqB, HB, 2, ac_s, "sqB", l)
                project_all("bo", xT)
                project_all("gb", xT)
                pe.wait_ge(*dv_s.at("hBo", l))
                project_all("pb", hB)
                pe.wait_ge(*dv_s.at("merged", l, 7))
                project_all("wo", merged)
                width_sums(l, "mu1", x1T, dv_s, "res1")
                width_sums(l, "var1", sqL, ac_s, "sq1")
                if l % 2 == 0:
                    pe.wait_ge(*ac_s.at("ln1", l, KC - 1))
                    with pe.Fori(0, FC // 2) as i:
                        for s in range(2):
                            pe.wait_ge(ff_in[s], 32 * i + 32)
                            w = ff_w1[s]
                            pe.wait_ge(ff_silu[s], i + 1)
                            for k in range(KC):
                                mm = nc.tensor.matmul(bank[2 * s][:, 0:T], w[:, 0, k, :], x1T[:, k, :],
                                                      start=k == 0, stop=k == KC - 1)
                            mm.then_inc(ff_gate[s], 1)
                            pe.wait_ge(ff_h[s], i + 1)
                            for k in range(KC):
                                mm = nc.tensor.matmul(bank[2 * s + 1][:, 0:T], w[:, 1, k, :], x1T[:, k, :],
                                                      start=k == 0, stop=k == KC - 1)
                            mm.then_inc(ff_up[s], 1)
                    for s in range(2):
                        pe.wait_ge(ff_h[s], FC // 2 + 1)
                    with pe.Fori(0, KC // 2) as i:
                        for s in range(2):
                            pe.wait_ge(ff_in2[s], 16 * i + 16)
                            pe.wait_ge(ff_res[s], i + 1)
                            for f in range(FC):
                                mm = nc.tensor.matmul(bank[4 + s][:, 0:T], ff_w2[s][:, f, :], hT[:, f, :],
                                                      start=f == 0, stop=f == FC - 1)
                            mm.then_inc(ff_down[s], 1)
                    for s in range(2):
                        pe.wait_ge(ff_res[s], KC // 2 + 1)
                    width_sums(l, "mu2", x1T)
                    width_sums(l, "var2", sqL, ac_s, "sq2")
                else:
                    tensor_moe(l)
                    width_sums(l, "mu2", acc)
                    width_sums(l, "var2", sqL, ac_s, "sq2")
            to_rows(1, "y", xT, ac_s, "ln2", 1, KC - 1)

        @block.scalar
        def _(act):
            for s in ff_silu:
                act.sem_inc(s, 1)

            def copy_out(l, dst, name, i, m, rows=P, cols=T, key=None):
                act.wait_ge(*pe_s.at("mm", l, name, i, m))
                nc.scalar.activation(dst, of(l, name, i, m)[0:rows, 0:cols], ACT.Copy)\
                    .then_inc(*free(ac_s, l, name, i, m))
                table[("act", "v", l, name, i, m)] = ac_s.count

            def evac(l, name, i, m):
                if name == "f":
                    copy_out(l, fP[i][:, m, :], name, i, m)
                elif name == "q":
                    copy_out(l, qA[i][:, m, :], name, i, m)
                elif name == "g":
                    copy_out(l, gS[:, 4 * i + m, :], name, i, m)
                elif name == "v":
                    r = TT[m][1]
                    copy_out(l, vTok[0:r, m, 512 * i:512 * i + 512], name, i, m, r, 512)
                elif name == "bv":
                    r = TT[m][1]
                    copy_out(l, vB[0:r, m, 512 * i:512 * i + 512], name, i, m, r, 512)
                elif name == "bu":
                    c = 4 * i + m
                    if c == 0:
                        act.wait_ge(*dv_s.at("qS", l, 0))
                    act.wait_ge(*pe_s.at("mm", l, name, i, m))
                    nc.scalar.activation(U[:, c, UP:UP + SEQ], of(l, name, i, m)[:, 0:SEQ], ACT.Copy)\
                        .then_inc(*ac_s.done())
                    nc.scalar.activation(U[:, c, UP + SEQ:].rearrange("p (b u) -> p b u", b=DB)[:, :, UP:],
                                         of(l, name, i, m)[:, SEQ:T].rearrange("p (b u) -> p b u", b=DB), ACT.Copy)\
                        .then_inc(*free(ac_s, l, name, i, m))

            def prepare(l, hf):
                if hf == 1:
                    act.wait_ge(*dv_s.at("qS", l, 0))
                nc.scalar.activation(kA, fP[hf], ACT.Sigmoid, scale=-1.0).then_inc(*ac_s.done())
                act.wait_ge(*ac_s.last())
                nc.scalar.activation(fP[hf], fP[hf], ACT.Sigmoid).then_inc(*ac_s.done("sigmoid", l, hf))
                nc.scalar.activation(qA[hf], qA[hf], ACT.Silu).then_inc(*ac_s.done("silu q", l, hf))
                act.wait_ge(*dv_s.at("f", l, hf))
                nc.scalar.activation(fP[hf], fP[hf], ACT.Ln).then_inc(*ac_s.done("log f", l, hf))

            def decays(l, hf, lv):
                h, n = 1 << lv, T if lv <= 2 else SEQ
                if lv == 0:
                    act.wait_ge(*ac_s.at("log f", l, hf))
                    act.wait_ge(*po_s.at("R", l, hf))
                else:
                    act.wait_ge(*po_s.at("update", l, hf, lv - 1))
                if lv >= 2:
                    act.wait_ge(*pe_s.at("level", l, hf, lv - 2, 1))
                elif hf == 1:
                    act.wait_ge(*pe_s.at("kt", l, 0, 2))
                nc.scalar.activation(half(blocks(Qe[lv % 2], h, n), 1, h), half(blocks(fP[hf], h, n), 1, h), ACT.Exp)\
                    .then_inc(*ac_s.done())
                nc.scalar.activation(half(blocks(Ke[lv % 2], h, n), 0, h), half(blocks(R, h, n), 0, h), ACT.Exp)\
                    .then_inc(*ac_s.done("exp", l, hf, lv))

            def key_end(l, hf):
                act.wait_ge(*po_s.at("update", l, hf, LEVELS - 1))
                act.wait_ge(*pe_s.at("level", l, hf, 6, 1))
                nc.scalar.activation(Ke[0], R, ACT.Exp).then_inc(*ac_s.done("exp end", l, hf))
                nc.scalar.activation(qS[:, 4 * hf:4 * hf + 4, :], fP[hf][:, :, SEQ:T], ACT.Exp).then_inc(*ac_s.done())
                nc.scalar.activation(decA[:, 4 * hf:4 * hf + 4, :], fP[hf][:, :, SEQ + DS - 1:T:DS], ACT.Exp)\
                    .then_inc(*ac_s.done("qS", l, hf))

            def norm(l, which, src, dst):
                for k in range(KC):
                    act.wait_ge(*dv_s.at("xc" + which, l, k))
                    nc.scalar.activation(sqL[:, k, :], src[:, k, :], ACT.Square).then_inc(*ac_s.done("sq" + which, l, k))
                act.wait_ge(*pe_s.at("var" + which, l))
                nc.scalar.activation(rstd, of(l, "var" + which)[:, 0:T], ACT.Sqrt, bias=eps, scale=1.0 / D)\
                    .then_inc(*free(ac_s, l, "var" + which))
                for k in range(KC):
                    act.wait_ge(*dv_s.at("nrm" + which, l, k))
                    nc.scalar.activation(dst[:, k, :], src[:, k, :], ACT.Identity,
                                         scale=par[:, k, PAR["g" + which] + l:PAR["g" + which] + l + 1],
                                         bias=par[:, k, PAR["b" + which] + l:PAR["b" + which] + l + 1])\
                        .then_inc(*ac_s.done("ln" + which, l, k))

            def experts(it0):
                with act.Fori(0, NE // 2) as pr:
                    it = it0 + pr

                    def columns_high(q):
                        s = q % 2
                        act.wait_ge(moe_in[s], 32 * (it * EST + q // 2) + 32)
                        act.wait_ge(mo_gu[s], it * EST + q // 2 + 1)
                        for i in range(2):
                            k = slice(4 * i, 4 * i + 4)
                            nc.scalar.activation(w1h[s][:, k], mo_w1[s][:, k], ACT.Copy).then_inc(mo_w1h[s], 1)

                    def down_high(q):
                        act.wait_ge(moe_in2[q % 2], 16 * (it * EST + q // 2) + 16)
                        if q < 2 * EST - 2:
                            act.wait_ge(mo_down[(q + 1) % 2], it * EST + (q + 1) // 2 + 1)
                        nc.scalar.activation(down_split(q)[0], mo_w2[q % 2], ACT.Copy).then_inc(mo_w2h[q % 2], 1)

                    def hidden_high(q):
                        act.wait_ge(mo_turn[q % 2], it * EST + q // 2 + 1)
                        nc.scalar.activation(hidh[q % 2], bank[2][:, 256 * (q % 2):256 * (q % 2) + 256]
                                             .rearrange("p (f t) -> p f t", f=2), ACT.Copy).then_inc(mo_hh[q % 2], 1)

                    def tokens_high(ei):
                        act.wait_ge(mo_gath[ei], it + 2)
                        for i in range(2):
                            nc.scalar.activation(xgh[ei][:, 4 * i:4 * i + 4, :],
                                                 bank[5 + i].rearrange("p (k t) -> p k t", k=4), ACT.Copy)\
                                .then_inc(mo_xh, 1)
                        nc.scalar.activation(gselT[ei], bank[7][:, 0:T], ACT.Copy).then_inc(mo_a, 1)

                    def outputs(ei):
                        p = (ei + 1) * EST - 1
                        act.wait_ge(mo_down[p % 2], it * EST + p // 2 + 2)
                        nc.scalar.activation(ysb[:, 0:512], bank[3], ACT.Copy).then_inc(mo_a, 1)
                        nc.scalar.activation(ysb[:, 512:], bank[4], ACT.Copy).then_inc(mo_ys, 1)

                    columns_high(0)
                    tokens_high(0)
                    for q in range(2 * EST + 2):
                        if 2 <= q < 2 * EST:
                            down_high(q - 2)
                        if q == 2 * EST - 1:
                            down_high(q - 1)
                        if q == 2 * EST:
                            down_high(q - 1)
                        if q == EST + 2:
                            outputs(0)
                        if q + 1 < 2 * EST:
                            columns_high(q + 1)
                        if q < 2 * EST:
                            act.wait_ge(mo_gu[q % 2], it * EST + q // 2 + 2)
                            nc.scalar.activation(sil[q % 2], bank[q % 2][:, 0:NG], ACT.Silu).then_inc(mo_sil[q % 2], 1)
                        if 1 <= q <= 2 * EST:
                            hidden_high(q - 1)
                        if q == GATHER_AT:
                            tokens_high(1)
                    outputs(1)

            def scalar_moe(l):
                for t, (t0, r) in enumerate(TT):
                    for i in range(2):
                        act.wait_ge(*pe_s.at("xt", l, t, i))
                        nc.scalar.activation(xtk[0:r, t, 512 * i:512 * i + 512], of(l, "xt", t, i)[0:r, :], ACT.Copy)\
                            .then_inc(*free(ac_s, l, "xt", t, i))
                table[("act", "xtk")] = ac_s.count
                act.wait_ge(*dv_s.at("less max"))
                nc.scalar.activation(expl, expl, ACT.Exp).then_inc(*ac_s.done("exp logits"))
                act.wait_ge(*dv_s.at("pos"))
                for n, c in (("cp", 16 * HB), ("n", 32), ("conv", 32)):
                    act.wait_ge(stored[n], c * (l + 1))
                experts(0)
                flag = act.value_load(over, min_val=0, max_val=1)
                with act.If(flag > 0):
                    with act.Fori(1, 3) as ps:
                        experts(ps * (NE // 2))

            act.dma_start(gbias[:, 0:2], I["b_ig"].rearrange("l h -> h l")).then_inc(load["bias"], 16)
            act.dma_start(gbias[:, 2:4], I["b_fg"].rearrange("l h -> h l")).then_inc(load["bias"], 16)
            act.dma_start(m0r, I["state_mlstm_m"].rearrange("l b h -> h l b")).then_inc(load["bias"], 16)
            for t, (t0, r) in enumerate(TT):
                for i in range(2):
                    act.wait_ge(*pe_s.at("xin", t, i))
                    nc.scalar.activation(xT[:, 4 * i:4 * i + 4, t0:t0 + r],
                                         of(0, "xin", t, i).rearrange("p (c t) -> p c t", c=4)[:, :, 0:r], ACT.Copy)\
                        .then_inc(*free(ac_s, 0, "xin", t, i))
            table[("act", "xT", 0)] = ac_s.count
            act.wait_ge(*pe_s.at("par"))
            nc.scalar.activation(par, of(0, "par")[:, 0:KC * NPAR].rearrange("p (c n) -> p c n", c=KC), ACT.Copy)\
                .then_inc(*free(ac_s, 0, "par"))
            table[("act", "par")] = ac_s.count
            act.wait_ge(*pe_s.at("scT"))
            nc.scalar.activation(scT, of(0, "scT")[:, 0:KC * 48].rearrange("p (c n) -> p c n", c=KC), ACT.Copy)\
                .then_inc(*free(ac_s, 0, "scT"))
            table[("act", "scT")] = ac_s.count
            act.wait_ge(*dv_s.at("lb max"))
            nc.scalar.activation(lbc[:, :, 0, :], lbc[:, :, 0, :], ACT.Exp).then_inc(*ac_s.done("lb exp"))

            for l in range(DEPTH):
                act.wait_ge(*pe_s.at("n0", l))
                nc.scalar.activation(n0T, of(l, "n0")[:, 0:64], ACT.Copy).then_inc(*free(ac_s, l, "n0"))
                table[("act", "n0T", l)] = ac_s.count
                for name in ("f", "q"):
                    for m in range(4):
                        evac(l, name, 0, m)
                tiles = {0: [("v", 0, t) for t in range(3)] + [(n, i, m) for n, i in (("g", 0), ("f", 1), ("q", 1)) for m in range(4)],
                         1: [("v", 1, t) for t in range(3)] + [(n, i, m) for n, i in (("g", 1), ("bu", 0), ("bu", 1)) for m in range(4)]
                         + [("bv", i, t) for i in range(2) for t in range(3)]}
                for hf in range(2):
                    todo = list(tiles[hf])

                    def step():
                        if todo:
                            evac(l, *todo.pop(0))

                    act.wait_ge(*ac_s.last())
                    prepare(l, hf)
                    step()
                    decays(l, hf, 0)
                    step()
                    for lv in range(-1, LEVELS):
                        if 0 <= lv < LEVELS - 1:
                            decays(l, hf, lv + 1)
                        step()
                        if lv == LEVELS - 1:
                            act.wait_ge(*pe_s.at("level", l, hf, 7, 0))
                            if hf == 1:
                                act.wait_ge(*pe_s.at("o", l, 0, 1))
                            nc.scalar.activation(attX, of(l, "level", hf, 7, 0).rearrange("p (j t) -> p j t", j=4), ACT.Copy)\
                                .then_inc(*free(ac_s, l, "level", hf, 7, 0))
                            table[("act", "cross", l, hf)] = ac_s.count
                    key_end(l, hf)
                    for t, (t0, r) in enumerate(TT):
                        act.wait_ge(*pe_s.at("kt", l, hf, t))
                        nc.scalar.activation(kTok[0:r, t, 512 * hf:512 * hf + 512], of(l, "kt", hf, t)[0:r, :], ACT.Copy)\
                            .then_inc(*free(ac_s, l, "kt", hf, t))
                        table[("act", "kt", l, hf, t)] = ac_s.count
                    step()
                    act.wait_ge(*pe_s.at("st", l, hf))
                    if 2 * l + hf > 0:
                        act.wait_ge(stored["st"], 16 * (2 * l + hf))
                    nc.scalar.activation(stP, of(l, "st", hf).rearrange("p (j v) -> p j v", j=4), ACT.Copy)\
                        .then_inc(*free(ac_s, l, "st", hf))
                    table[("act", "st", l, hf)] = ac_s.count
                    while todo:
                        step()
                act.wait_ge(load["bias"], 48)
                for g in range(2):
                    act.wait_ge(*pe_s.at("gate", l, g))
                    nc.scalar.activation(rows[g], of(l, "gate", g)[0:HB, 0:T], ACT.Identity,
                                         bias=gbias[:, 2 * g + l:2 * g + l + 1]).then_inc(*free(ac_s, l, "gate", g))
                table[("act", "gates", l)] = ac_s.count
                act.wait_ge(*dv_s.at("abs f", l))
                nc.scalar.activation(rows[4], rows[4], ACT.Exp, scale=-1.0).then_inc(*ac_s.done("exp f", l))
                act.wait_ge(*dv_s.at("one plus", l))
                nc.scalar.activation(rows[2], rows[5], ACT.Ln).then_inc(*ac_s.done("ln f", l))
                act.wait_ge(*dv_s.at("rows", l))
                nc.scalar.activation(bcr, bcr, ACT.Exp).then_inc(*ac_s.done("bcr", l))
                nc.scalar.activation(rows[5], rows[5], ACT.Exp).then_inc(*ac_s.done("wst", l))
                nc.scalar.activation(gS, gS, ACT.Silu).then_inc(*ac_s.done("silu g", l))
                act.wait_ge(*dv_s.at("conv", l))
                nc.scalar.activation(uS, uS, ACT.Silu).then_inc(*ac_s.done("silu u", l))
                for i in range(2):
                    act.wait_ge(*pe_s.at("cv", l, i))
                    if l > 0 and i == 0:
                        act.wait_ge(stored["conv"], 32 * l)
                    nc.scalar.activation(cvo[:, 512 * i:512 * i + 512], of(l, "cv", i)[0:27, :], ACT.Copy)\
                        .then_inc(*free(ac_s, l, "cv", i))
                table[("act", "cvo", l)] = ac_s.count
                for c in range(KC):
                    act.wait_ge(*pe_s.at("qB", l, c))
                    nc.scalar.activation(qB[:, c, :], of(l, "qB", c)[:, 0:T], ACT.Copy).then_inc(*free(ac_s, l, "qB", c))
                    act.wait_ge(*pe_s.at("kB", l, c))
                    nc.scalar.activation(kB[:, c, :], of(l, "kB", c)[:, 0:T], ACT.Copy, scale=256 ** -0.5)\
                        .then_inc(*free(ac_s, l, "kB", c))
                    table[("act", "qkB", l, c)] = ac_s.count
                act.wait_ge(*pe_s.at("col", l))
                if l > 0:
                    act.wait_ge(*dv_s.at("nS", l - 1, HB - 1))
                nc.scalar.activation(colA[:, 0:2, :], of(l, "col")[:, 0:16].rearrange("p (t n) -> p t n", t=2), ACT.Copy)\
                    .then_inc(*ac_s.done())
                nc.scalar.activation(colA[0:NS, 2, :], of(l, "col")[0:NS, 16:24], ACT.Copy).then_inc(*free(ac_s, l, "col"))
                table[("act", "colA", l)] = ac_s.count
                for h in range(HB):
                    act.wait_ge(*pe_s.at("spread", l, h, 1))
                    if h >= 2:
                        act.wait_ge(*dv_s.at("nS", l, h - 2))
                    elif l > 0:
                        act.wait_ge(*dv_s.at("nS", l - 1, HB - 1))
                    nc.scalar.activation(eb[h % 2], of(l, "spread", h, 1)[:, 0:T + NS + DB], ACT.Copy)\
                        .then_inc(*free(ac_s, l, "spread", h, 1))
                    table[("act", "eb", l, h)] = ac_s.count
                    act.wait_ge(*dv_s.at("w", l, h))
                    nc.scalar.activation(wW[h % 2][:, 0:384], wW[h % 2][:, 0:384], ACT.Exp, scale=-1.0)\
                        .then_inc(*ac_s.done())
                    nc.scalar.activation(wW[h % 2][0:NS, 384:448], wW[h % 2][0:NS, 384:448], ACT.Exp, scale=-1.0)\
                        .then_inc(*ac_s.done("ew", l, h))
                    act.wait_ge(*pe_s.at("cP", l, h))
                    if l * HB + h > 0:
                        act.wait_ge(stored["cp"], 16 * (l * HB + h))
                    nc.scalar.activation(cP, of(l, "cP", h).rearrange("p (c v) -> p c v", c=2), ACT.Copy)\
                        .then_inc(*free(ac_s, l, "cP", h))
                    table[("act", "cPo", l, h)] = ac_s.count
                act.wait_ge(*dv_s.at("oS", l))
                act.wait_ge(*dv_s.at("nS", l, HB - 1))
                nc.scalar.activation(sqA, oA, ACT.Square).then_inc(*ac_s.done("sqA", l))
                for h in range(HA):
                    act.wait_ge(*pe_s.at("rms", l, h))
                    nc.scalar.activation(rsA[:, h, :], of(l, "rms", h)[:, 0:T], ACT.Sqrt, bias=eps, scale=1.0 / P)\
                        .then_inc(*free(ac_s, l, "rms", h))
                table[("act", "rsA", l)] = ac_s.count
                act.wait_ge(*pe_s.at("interB", l, DB - 1))
                for i in range(2):
                    nc.scalar.activation(interS[:, i, :], of(l, "interB", i)[0:NS, :], ACT.Copy)\
                        .then_inc(*free(ac_s, l, "interB", i))
                act.wait_ge(*pe_s.at("nrow", l))
                if l > 0:
                    act.wait_ge(stored["n"], 32 * l)
                nc.scalar.activation(nrow, of(l, "nrow")[0:64, 0:P], ACT.Copy).then_inc(*ac_s.done())
                nc.scalar.activation(nrowP, of(l, "nrow")[0:8, P:2 * P], ACT.Copy).then_inc(*free(ac_s, l, "nrow"))
                table[("act", "nro", l)] = ac_s.count
                act.wait_ge(*dv_s.at("xcB", l, HB - 1))
                nc.scalar.activation(sqB, hB, ACT.Square).then_inc(*ac_s.done("sqB", l))
                for i in range(2):
                    for m in range(4):
                        act.wait_ge(*pe_s.at("mm", l, "ga", i, m))
                        if 4 * i + m >= 2:
                            act.wait_ge(*dv_s.at("yA", l, 4 * i + m - 2))
                        nc.scalar.activation(tg[m % 2], of(l, "ga", i, m)[:, 0:T], ACT.Sigmoid)\
                            .then_inc(*free(ac_s, l, "ga", i, m))
                        table[("act", "ga", l, 4 * i + m)] = ac_s.count
                for h in range(HB):
                    act.wait_ge(*pe_s.at("varB", l, h))
                    nc.scalar.activation(rsB[:, h, :], of(l, "varB", h)[:, 0:T], ACT.Sqrt, bias=eps, scale=1.0 / 256)\
                        .then_inc(*free(ac_s, l, "varB", h))
                table[("act", "rsB", l)] = ac_s.count
                act.wait_ge(*dv_s.at("oA", l))
                for name, dst in (("bo", boS), ("gb", gbS)):
                    for i in range(2):
                        for m in range(4):
                            act.wait_ge(*pe_s.at("mm", l, name, i, m))
                            nc.scalar.activation(dst[:, 4 * i + m, :], of(l, name, i, m)[:, 0:T], ACT.Sigmoid)\
                                .then_inc(*free(ac_s, l, name, i, m))
                    table[("act", name, l)] = ac_s.count
                norm(l, "1", x1T, x1T)
                if l % 2 == 0:
                    with act.Fori(0, FC // 2) as i:
                        for s in range(2):
                            act.wait_ge(ff_gate[s], i + 1)
                            act.wait_ge(ff_h[s], i + 1)
                            nc.scalar.activation(silu[s], bank[2 * s][:, 0:T], ACT.Silu).then_inc(ff_silu[s], 1)
                    norm(l, "2", x1T, xT)
                else:
                    scalar_moe(l)
                    norm(l, "2", acc, xT)
            for t, (t0, r) in enumerate(TT):
                for i in range(2):
                    act.wait_ge(*pe_s.at("y", 1, t, i))
                    nc.scalar.activation(yrow[0:r, t, 512 * i:512 * i + 512], of(1, "y", t, i)[0:r, :], ACT.Copy)\
                        .then_inc(*free(ac_s, 1, "y", t, i))
            table[("act", "y")] = ac_s.count

        @block.vector
        def _(dve):
            for s in ff_h + ff_res + mo_h + mo_w1l + mo_w2l + mo_hl + [mo_acc, mo_shift]:
                dve.sem_inc(s, 1)

            def col(name, l, k, n=0):
                return par[:, k, PAR[name] + l + n:PAR[name] + l + n + 1]

            def settle():
                dve.wait_ge(*dv_s.last())

            dve.wait_ge(*po_s.at("iota"))
            nc.vector.tensor_tensor(xorI, colI, rowI, ALU.bitwise_xor).then_inc(*dv_s.done())
            nc.vector.tensor_tensor(laterT, colI, rowI, ALU.is_gt).then_inc(*dv_s.done())
            nc.vector.tensor_tensor(causal, colI, rowI, ALU.is_ge).then_inc(*dv_s.done())
            nc.vector.tensor_scalar(row3, rowI[:, 0:1], 3, None, ALU.logical_shift_right).then_inc(*dv_s.done())
            nc.vector.tensor_scalar(row2, rowI[:, 0:1], 2, None, ALU.logical_shift_right).then_inc(*dv_s.done())
            settle()
            nc.vector.tensor_copy(xorF, xorI).then_inc(*dv_s.done())
            nc.vector.tensor_tensor(seg, colI[:, 0:DB], row3.broadcast_to([P, DB]), ALU.is_equal).then_inc(*dv_s.done())
            nc.vector.tensor_tensor(blk4, colI[:, 0:32], row2.broadcast_to([P, 32]), ALU.is_equal).then_inc(*dv_s.done())
            dve.wait_ge(*po_s.at("ident"))
            for h in range(HB):
                nc.vector.tensor_copy(sel[:, h, :], ident[0:HB, h:h + 1].broadcast_to([HB, P])).then_inc(*dv_s.done())
            settle()
            nc.vector.scalar_tensor_tensor(own8, xorF[:, 0:64], float(DS), causal[:, 0:64], ALU.is_lt, ALU.mult)\
                .then_inc(*dv_s.done())
            settle()
            nc.vector.tensor_tensor(xorF, xorF, laterT, ALU.mult).then_inc(*dv_s.done())
            settle()
            for lv in range(7):
                settle()
                nc.vector.tensor_scalar(maskt, xorF, float(2 << lv), None, ALU.is_lt).then_inc(*dv_s.done())
                settle()
                nc.vector.scalar_tensor_tensor(levelm[:, lv, :], xorF, float(1 << lv), maskt, ALU.is_ge, ALU.mult)\
                    .then_inc(*dv_s.done())
            table[("dve", "masks")] = dv_s.count
            dve.wait_ge(*ac_s.at("par"))
            nc.vector.tensor_tensor(lbt, par[:, :, 0], par[:, :, 1], ALU.max).then_inc(*dv_s.done())
            settle()
            for l in range(DEPTH):
                nc.vector.tensor_tensor(lbc[:, l, 0, :], par[:, :, l], lbt, ALU.subtract).then_inc(*dv_s.done("lb max"))
            dve.wait_ge(*ac_s.at("lb exp"))
            nc.vector.tensor_tensor(lbt, lbc[:, 0, 0, :], lbc[:, 1, 0, :], ALU.add).then_inc(*dv_s.done())
            settle()
            nc.vector.reciprocal(lbt, lbt).then_inc(*dv_s.done())
            settle()
            nc.vector.tensor_tensor(lbc[:, 1, 0, :], lbc[:, 1, 0, :], lbt, ALU.mult).then_inc(*dv_s.done())
            nc.vector.memset(lbc[:, 0, 0, :], 0.0).then_inc(*dv_s.done())
            settle()
            nc.vector.tensor_scalar(lbc[:, :, 1, :], lbc[:, :, 0, :], -1.0, 1.0, ALU.mult, ALU.add).then_inc(*dv_s.done())
            settle()

            def prepare(l, hf):
                dve.wait_ge(*ac_s.at("sigmoid", l, hf))
                for j in range(4):
                    h = 4 * hf + j
                    nc.vector.tensor_scalar(fP[hf][:, j, :], fP[hf][:, j, :], lbc[:, l, 1, h:h + 1], lbc[:, l, 0, h:h + 1],
                                            ALU.mult, ALU.add).then_inc(*dv_s.done())
                settle()
                nc.vector.tensor_scalar(fP[hf], fP[hf], TINY, None, ALU.max).then_inc(*dv_s.done("f", l, hf))
                for j in range(4):
                    h = 4 * hf + j
                    nc.vector.tensor_scalar(kA[:, j, :], kA[:, j, :], lbc[:, l, 1, h:h + 1], None, ALU.mult)\
                        .then_inc(*dv_s.done("prep", l, hf))

            def operands(l, hf, lv):
                h, n = 1 << lv, T if lv <= 2 else SEQ
                dve.wait_ge(*ac_s.at("exp", l, hf, lv))
                for dst, src, side in ((Qe[lv % 2], qA[hf], 1), (Ke[lv % 2], kA, 0)):
                    d, s = half(blocks(dst, h, n), side, h), half(blocks(src, h, n), side, h)
                    nc.vector.tensor_tensor(d, d, s, ALU.mult).then_inc(*dv_s.done("operands", l, hf, lv))

            def collect(l, hf, lv):
                if lv == -1 and hf == 1:
                    dve.wait_ge(*pe_s.at("o", l, 0, 1))
                for t in range(3 if lv <= 2 else 2):
                    r = TT[t][1]
                    dve.wait_ge(*pe_s.at("level", l, hf, lv, t))
                    src = of(l, "level", hf, lv, t)[0:r, 0:4 * r].rearrange("p (j t) -> p j t", j=4)
                    dst = attD[:, t] if t < 2 else attS[:, 4 * hf:4 * hf + 4, :]
                    if lv < 0:
                        nc.vector.tensor_tensor(dst, src, ident[0:r, 0:r].unsqueeze(1).broadcast_to([r, 4, r]), ALU.mult)\
                            .then_inc(*free(dv_s, l, "level", hf, lv, t))
                    else:
                        nc.vector.copy_predicated(dst, levelm[0:r, lv, 0:r].unsqueeze(1).broadcast_to([r, 4, r]), src)\
                            .then_inc(*free(dv_s, l, "level", hf, lv, t))
                table[("dve", "att", l, hf)] = dv_s.count

            def norm(l, which, src):
                dve.wait_ge(*pe_s.at("mu" + which, l))
                for k in range(KC):
                    ins = nc.vector.scalar_tensor_tensor(src[:, k, :], of(l, "mu" + which)[:, 0:T], -1.0 / D, src[:, k, :],
                                                         ALU.mult, ALU.add)
                    if k < KC - 1:
                        ins.then_inc(*dv_s.done("xc" + which, l, k))
                ins.then_inc(*free(dv_s, l, "mu" + which))
                table[("dve", "xc" + which, l, KC - 1)] = dv_s.count
                dve.wait_ge(*ac_s.at("free", l, "var" + which))
                nc.vector.reciprocal(rstd, rstd).then_inc(*dv_s.done())
                settle()
                for k in range(KC):
                    nc.vector.tensor_tensor(src[:, k, :], src[:, k, :], rstd, ALU.mult).then_inc(*dv_s.done("nrm" + which, l, k))

            def experts(it0):
                with dve.Fori(0, NE // 2) as pr:
                    it = it0 + pr

                    def select(ei):
                        e = 2 * pr + ei
                        dve.wait_ge(mo_gath[ei], it + 1)
                        for t in range(3):
                            ins = nc.vector.tensor_scalar(selm[ei][:, t, :], iotaF, pos[:, t, bass.ds(e, 1)], None, ALU.is_equal)
                            ins.then_inc(*((mo_v, 1) if t < 2 else (mo_sel[ei], 1)))
                        for t in range(3):
                            ins = nc.vector.tensor_scalar(gsel[ei][:, t, :], iotaF, pos[:, t, bass.ds(e, 1)],
                                                          gate[:, t, bass.ds(e, 1)], ALU.is_equal, ALU.mult)
                            ins.then_inc(*((mo_v, 1) if t < 2 else (mo_gsel[ei], 1)))

                    def columns_rest(q):
                        s = q % 2
                        for i in range(2):
                            k = slice(4 * i, 4 * i + 4)
                            dve.wait_ge(mo_w1h[s], 2 * (it * EST + q // 2) + i + 1)
                            ins = nc.vector.tensor_tensor(w1l[s][:, k], mo_w1[s][:, k], w1h[s][:, k], ALU.subtract)
                            ins.then_inc(*((mo_v, 1) if i == 0 else (mo_w1l[s], 1)))

                    def down_rest(q):
                        dve.wait_ge(mo_w2h[q % 2], it * EST + q // 2 + 1)
                        high, rest = down_split(q)
                        nc.vector.tensor_tensor(rest, mo_w2[q % 2], high, ALU.subtract).then_inc(mo_w2l[q % 2], 1)

                    def hidden_rest(q):
                        dve.wait_ge(mo_hh[q % 2], it * EST + q // 2 + 1)
                        nc.vector.tensor_tensor(hidl[q % 2], bank[2][:, 256 * (q % 2):256 * (q % 2) + 256]
                                                .rearrange("p (f t) -> p f t", f=2), hidh[q % 2], ALU.subtract)\
                            .then_inc(mo_hl[q % 2], 1)

                    def tokens_rest(ei):
                        for i in range(2):
                            dve.wait_ge(mo_xh, 2 * (2 * it + ei) + i + 1)
                            ins = nc.vector.tensor_tensor(xgl[ei][:, 4 * i:4 * i + 4, :],
                                                          bank[5 + i].rearrange("p (k t) -> p k t", k=4),
                                                          xgh[ei][:, 4 * i:4 * i + 4, :], ALU.subtract)
                            ins.then_inc(*((mo_v, 1) if i == 0 else (mo_xg, 1)))

                    def add(ei):
                        x = 2 * it + ei
                        dve.wait_ge(mo_acc, 8 * x + 1)
                        for c in range(KC):
                            dve.wait_ge(mo_sc, 8 * x + c + 1)
                            nc.vector.tensor_tensor(acc[:, c, :], acc[:, c, :], bank[(7, 5, 6)[c % 3]][:, 0:T], ALU.add)\
                                .then_inc(mo_acc, 1)

                    select(0)
                    columns_rest(0)
                    tokens_rest(0)
                    for q in range(2 * EST + 2):
                        if 2 <= q < 2 * EST:
                            down_rest(q - 2)
                        if q == 2 * EST - 1:
                            down_rest(q - 1)
                        if q == 2 * EST:
                            down_rest(q - 1)
                        if q + 1 < 2 * EST:
                            columns_rest(q + 1)
                        if q == 2:
                            select(1)
                        if q < 2 * EST:
                            dve.wait_ge(mo_sil[q % 2], it * EST + q // 2 + 1)
                            nc.vector.tensor_tensor(hid[q % 2], sil[q % 2], bank[q % 2][:, NG:2 * NG], ALU.mult)\
                                .then_inc(mo_h[q % 2], 1)
                        if 1 <= q <= 2 * EST:
                            hidden_rest(q - 1)
                        if q == GATHER_AT:
                            tokens_rest(1)
                        if q == SCATTER_AT:
                            add(0)
                    add(1)

            def vector_moe(l):
                dve.wait_ge(*ac_s.at("ln1", l, KC - 1))
                nc.vector.tensor_scalar(acc, x1T, ALPHA, None, ALU.mult).then_inc(*dv_s.done())
                nc.vector.memset(lg, 0.0).then_inc(*dv_s.done())
                nc.vector.memset(xtk[NS:P, 2, :], 0.0).then_inc(*dv_s.done())
                nc.vector.tensor_tensor(after_, causal, ident, ALU.subtract).then_inc(*dv_s.done())
                dve.wait_ge(*po_s.at("moe"))
                nc.vector.tensor_copy(iotaF, iotaI).then_inc(*dv_s.done())
                settle()
                dve.wait_ge(*pe_s.at("logits"))
                lgp = of(l, "logits")
                nc.vector.tensor_tensor(lg[:, 0:2, :], lgp[:, 0:2 * NE].rearrange("p (t e) -> p t e", t=2),
                                        brt.unsqueeze(1).broadcast_to([P, 2, NE]), ALU.add).then_inc(*dv_s.done())
                nc.vector.tensor_tensor(lg[0:NS, 2, :], lgp[0:NS, 2 * NE:3 * NE], brt[0:NS, :], ALU.add)\
                    .then_inc(*free(dv_s, l, "logits"))
                settle()
                le = lg.unsqueeze(3).broadcast_to([P, 3, NE, NE])
                lj = lg.unsqueeze(2).broadcast_to([P, 3, NE, NE])
                nc.vector.tensor_tensor(cmp1, lj, le, ALU.is_gt).then_inc(*dv_s.done())
                nc.vector.tensor_tensor(cmp2, lj, le, ALU.is_equal).then_inc(*dv_s.done())
                nc.vector.tensor_reduce(mx3, lg, AX.X, ALU.max).then_inc(*dv_s.done())
                settle()
                nc.vector.tensor_tensor(cmp2, cmp2, tri8.unsqueeze(1).broadcast_to([P, 3, NE, NE]), ALU.mult)\
                    .then_inc(*dv_s.done())
                nc.vector.tensor_tensor(expl, lg, mx3.unsqueeze(2).broadcast_to([P, 3, NE]), ALU.subtract)\
                    .then_inc(*dv_s.done("less max"))
                settle()
                nc.vector.tensor_tensor(cmp1, cmp1, cmp2, ALU.add).then_inc(*dv_s.done())
                settle()
                nc.vector.tensor_reduce(chosen, cmp1, AX.X, ALU.add).then_inc(*dv_s.done())
                settle()
                nc.vector.tensor_scalar(chosen, chosen, 2.0, None, ALU.is_lt).then_inc(*dv_s.done("chosen"))
                settle()
                dve.wait_ge(*ac_s.at("exp logits"))
                nc.vector.tensor_tensor(gate, expl, chosen, ALU.mult).then_inc(*dv_s.done())
                settle()
                nc.vector.tensor_reduce(mx3, gate, AX.X, ALU.add).then_inc(*dv_s.done())
                settle()
                nc.vector.reciprocal(mx3, mx3).then_inc(*dv_s.done())
                settle()
                nc.vector.tensor_tensor(gate, gate, mx3.unsqueeze(2).broadcast_to([P, 3, NE]), ALU.mult).then_inc(*dv_s.done())
                nc.vector.memset(pos, 0.0).then_inc(*dv_s.done())
                settle()
                dve.wait_ge(*pe_s.at("ranks"))
                rk = of(l, "ranks")
                nc.vector.scalar_tensor_tensor(pos[:, 0:2, :], rk[:, 0:2 * NE].rearrange("p (t e) -> p t e", t=2), 1.0,
                                               chosen[:, 0:2, :], ALU.add, ALU.mult).then_inc(*dv_s.done())
                nc.vector.scalar_tensor_tensor(pos[0:NS, 2, :], rk[0:NS, 2 * NE:3 * NE], 1.0, chosen[0:NS, 2, :],
                                               ALU.add, ALU.mult).then_inc(*dv_s.done())
                nc.vector.tensor_reduce(cnt, rk[:, 24:32], AX.X, ALU.max).then_inc(*free(dv_s, l, "ranks"))
                settle()
                nc.vector.tensor_scalar(over_all, cnt, float(BLOCK), None, ALU.is_gt).then_inc(*dv_s.done())
                nc.vector.tensor_scalar(pos, pos, -1.0, None, ALU.add).then_inc(*dv_s.done("pos"))
                settle()
                for n, c in (("cp", 16 * HB), ("n", 32), ("conv", 32)):
                    dve.wait_ge(stored[n], c * (l + 1))
                experts(0)
                flag = dve.value_load(over, min_val=0, max_val=1)
                with dve.If(flag > 0):
                    with dve.Fori(1, 3) as ps:
                        dve.wait_ge(mo_acc, NE * KC * ps + 1)
                        dve.wait_ge(mo_shift, ps)
                        nc.vector.tensor_scalar(pos, pos, -float(BLOCK), None, ALU.add).then_inc(mo_shift, 1)
                        dve.wait_ge(mo_shift, ps + 1)
                        nc.vector.tensor_copy(cnt, cnt)
                        experts(ps * (NE // 2))
                    dve.wait_ge(mo_acc, 3 * NE * KC + 1)
                dve.wait_ge(mo_acc, NE * KC + 1)

            for l in range(DEPTH):
                for hf in range(2):
                    prepare(l, hf)
                    settle()
                    for lv in range(LEVELS):
                        operands(l, hf, lv)
                        collect(l, hf, lv - 1)
                        settle()
                    dve.wait_ge(*ac_s.at("exp end", l, hf))
                    nc.vector.tensor_tensor(Ke[0], Ke[0], kA, ALU.mult).then_inc(*dv_s.done("key end", l, hf))
                    dve.wait_ge(*ac_s.at("qS", l, hf))
                    q = qS[:, 4 * hf:4 * hf + 4, :]
                    nc.vector.tensor_tensor(q, q, qA[hf][:, :, SEQ:T], ALU.mult).then_inc(*dv_s.done("qS", l, hf))
                    for t in range(2):
                        dve.wait_ge(*pe_s.at("o", l, hf, t))
                        nc.vector.tensor_copy(oA[:, 4 * hf:4 * hf + 4, t * P:(t + 1) * P],
                                              of(l, "o", hf, t).rearrange("p (j t) -> p j t", j=4))\
                            .then_inc(*free(dv_s, l, "o", hf, t))
                    if hf == 0:
                        if l > 0:
                            dve.wait_ge(stored["cp"], 16 * HB * l)
                        else:
                            nc.vector.memset(vB[NS:P, 2, :], 0.0).then_inc(*dv_s.done())
                        nc.vector.memset(kTok[NS:P, 2, :], 0.0).then_inc(*dv_s.done())
                        nc.vector.memset(vTok[NS:P, 2, :], 0.0).then_inc(*dv_s.done("rows padded", l))
                dve.wait_ge(*ac_s.at("free", l, "bu", 1, 3))
                dve.wait_ge(*po_s.at("U", l))
                dve.wait_ge(*pe_s.at("level", l, 1, 7, 0))
                for j in range(CW):
                    for c in range(KC):
                        us = uS[:, c, SEQ:T].rearrange("p (b t) -> p b t", b=DB)
                        uw = U[:, c, UP + SEQ:].rearrange("p (b u) -> p b u", b=DB)[:, :, j:j + DS]
                        w = par[:, c, PAR["cw"] + 4 * l + j:PAR["cw"] + 4 * l + j + 1]
                        for dst, src in ((uS[:, c, 0:SEQ], U[:, c, j:j + SEQ]), (us, uw)):
                            if j == 0:
                                ins = nc.vector.tensor_scalar(dst, src, w, col("cb", l, c), ALU.mult, ALU.add)
                            else:
                                ins = nc.vector.scalar_tensor_tensor(dst, src, w, dst, ALU.mult, ALU.add)
                            ins.then_inc(*dv_s.done("conv", l))
                    settle()
                dve.wait_ge(*ac_s.at("gates", l))
                nc.vector.scalar_tensor_tensor(rows[4], rows[1], -1.0, rows[1], ALU.mult, ALU.max).then_inc(*dv_s.done("abs f", l))
                dve.wait_ge(*ac_s.at("exp f", l))
                nc.vector.tensor_scalar(rows[5], rows[4], 1.0, None, ALU.add).then_inc(*dv_s.done("one plus", l))
                settle()
                nc.vector.scalar_tensor_tensor(rows[3], rows[5], -1.0, rows[4], ALU.add, ALU.subtract).then_inc(*dv_s.done())
                dve.wait_ge(*ac_s.at("ln f", l))
                settle()
                nc.vector.reciprocal(rows[5], rows[5]).then_inc(*dv_s.done())
                settle()
                nc.vector.tensor_tensor(rows[3], rows[3], rows[5], ALU.mult).then_inc(*dv_s.done())
                settle()
                nc.vector.tensor_tensor(rows[2], rows[2], rows[3], ALU.subtract).then_inc(*dv_s.done())
                settle()
                nc.vector.scalar_tensor_tensor(rows[1], rows[1], 0.0, rows[2], ALU.min, ALU.subtract).then_inc(*dv_s.done())
                settle()
                nc.vector.tensor_tensor_scan(rows[4], keep, rows[1], 0.0, ALU.mult, ALU.add).then_inc(*dv_s.done())
                settle()
                nc.vector.tensor_tensor(rows[2], rows[0], rows[4], ALU.subtract).then_inc(*dv_s.done())
                settle()
                nc.vector.tensor_copy(rows[5], rows[2]).then_inc(*dv_s.done())
                settle()
                nc.vector.tensor_scalar(rows[5][:, 0:1], rows[2][:, 0:1], 0.0, None, ALU.max).then_inc(*dv_s.done())
                nc.vector.tensor_tensor(rows[5][:, SEQ:T:DS], rows[2][:, SEQ:T:DS], m0r[:, l, :], ALU.max)\
                    .then_inc(*dv_s.done())
                settle()
                nc.vector.tensor_tensor_scan(rows[3], drop, rows[5], 0.0, ALU.add, ALU.max).then_inc(*dv_s.done())
                settle()
                Ml = rows[3][:, SEQ + DS - 1:T:DS]
                bl = rows[4][:, SEQ + DS - 1:T:DS]
                m3 = m0r[:, l, :].unsqueeze(2).broadcast_to([HB, DB, DS])
                if l > 0:
                    dve.wait_ge(stored["m"], 32 * l)
                nc.vector.tensor_tensor(mout[:, 0:DB], Ml, bl, ALU.add).then_inc(*dv_s.done())
                nc.vector.tensor_tensor(mout[:, DB:DB + 1], rows[3][:, SEQ - 1:SEQ], rows[4][:, SEQ - 1:SEQ], ALU.add)\
                    .then_inc(*dv_s.done("mout", l))
                dve.wait_ge(stored["st"], 16 * (2 * l + 2))
                nc.vector.scalar_tensor_tensor(bcr[:, 0:T], rows[4], -1.0, rows[3], ALU.mult, ALU.subtract)\
                    .then_inc(*dv_s.done())
                nc.vector.tensor_tensor(bcr[:, T:T + NS].rearrange("p (b t) -> p b t", b=DB), m3,
                                        rows[3][:, SEQ:T].rearrange("p (b t) -> p b t", b=DB), ALU.subtract)\
                    .then_inc(*dv_s.done())
                nc.vector.tensor_tensor(bcr[:, T + NS:], m0r[:, l, :], Ml, ALU.subtract).then_inc(*dv_s.done())
                nc.vector.tensor_scalar(rows[5][:, 0:SEQ], rows[2][:, 0:SEQ], rows[3][:, SEQ - 1:SEQ], None, ALU.subtract)\
                    .then_inc(*dv_s.done())
                nc.vector.tensor_tensor(rows[5][:, SEQ:T].rearrange("p (b t) -> p b t", b=DB),
                                        rows[2][:, SEQ:T].rearrange("p (b t) -> p b t", b=DB),
                                        Ml.unsqueeze(2).broadcast_to([HB, DB, DS]), ALU.subtract)\
                    .then_inc(*dv_s.done("rows", l))
                for b in range(DB):
                    s0 = strip_at(l, "S", b // 4)[0].rearrange("p (b h v) -> p b h v", b=4, h=HA)
                    dve.wait_ge(*pe_s.at("inter", l, b))
                    for q in range(2):
                        dve.wait_ge(*pe_s.at("dS", l, b, q))
                        for j in range(4):
                            h = 4 * q + j
                            s = s0[:, b % 4, h, :]
                            ins = nc.vector.scalar_tensor_tensor(s, s, decA[:, h, b:b + 1], of(l, "dS", b, q)[:, chunk(j)],
                                                                 ALU.mult, ALU.add)
                            if j < 3:
                                ins.then_inc(*dv_s.done())
                        ins.then_inc(*free(dv_s, l, "dS", b, q))
                    table[("dve", "newS", l, b)] = dv_s.count
                dve.wait_ge(*pe_s.at("inter", l, DB - 1))
                nc.vector.tensor_copy(oA[:, :, SEQ:T], of(l, "oS").rearrange("p (h t) -> p h t", h=HA))\
                    .then_inc(*free(dv_s, l, "oS"))
                table[("dve", "oS", l)] = dv_s.count
                nc.vector.tensor_copy(cvg[:, :, 0:UP], U[:, :, SEQ:SEQ + UP]).then_inc(*dv_s.done())
                nc.vector.tensor_copy(cvg[:, :, UP:27].rearrange("p c (b r) -> p c b r", b=DB),
                                      U[:, :, UP + SEQ:].rearrange("p c (b u) -> p c b u", b=DB)[:, :, :, DS:US])\
                    .then_inc(*dv_s.done("cvg", l))
                settle()
                nc.vector.memset(kTB[NS:P, 2, :], 0.0).then_inc(*dv_s.done("keys padded", l))
                dve.wait_ge(load["w4"], 32 * (l + 1))
                for dst, w4 in ((bdq, wq4), (bdk, wk4)):
                    nc.vector.tensor_tensor(dst.rearrange("p c (n j) -> p c n j", n=32),
                                            w4.unsqueeze(2).broadcast_to([P, KC, 32, 4]),
                                            blk4.unsqueeze(1).unsqueeze(3).broadcast_to([P, KC, 32, 4]), ALU.mult)\
                        .then_inc(*dv_s.done("bd", l))
                dve.wait_ge(*ac_s.at("colA", l))
                dve.wait_ge(*ac_s.at("n0T", l))
                for h in range(HB):
                    w, s = wW[h % 2], sW[h % 2]
                    dve.wait_ge(*pe_s.at("spread", l, h, 0))
                    Mb = of(l, "spread", h, 0)
                    nc.vector.tensor_scalar(w[:, 0:256], Mb[:, 0:256], colA[:, 0, h:h + 1], 0.0, ALU.subtract, ALU.max)\
                        .then_inc(*dv_s.done())
                    nc.vector.tensor_scalar(w[:, 256:384], Mb[:, 128:256], colA[:, 1, h:h + 1], 0.0, ALU.subtract, ALU.max)\
                        .then_inc(*dv_s.done())
                    nc.vector.tensor_scalar(w[0:NS, 384:448], Mb[0:NS, 256:320], colA[0:NS, 2, h:h + 1], 0.0,
                                            ALU.subtract, ALU.max).then_inc(*free(dv_s, l, "spread", h, 0))
                    table[("dve", "w", l, h)] = dv_s.count
                    dve.wait_ge(*ac_s.at("eb", l, h))
                    q3 = qI[:, 2 * h:2 * h + 2, :]
                    nc.vector.tensor_tensor(q3, qB[:, 2 * h:2 * h + 2, SEQ:T],
                                            eb[h % 2][:, T:T + NS].unsqueeze(1).broadcast_to([P, 2, NS]), ALU.mult)\
                        .then_inc(*dv_s.done())
                    nc.vector.tensor_copy(decB[:, h, :], eb[h % 2][:, T + NS:]).then_inc(*dv_s.done())
                    settle()
                    n0v = n0T.rearrange("p (b h c) -> p h c b", b=DB, h=HB)[:, h]
                    nc.vector.tensor_tensor(qn[:, 2 * h:2 * h + 2, :].rearrange("p c (b t) -> p c b t", b=DB),
                                            q3.rearrange("p c (b t) -> p c b t", b=DB),
                                            n0v.unsqueeze(3).broadcast_to([P, 2, DB, DS]), ALU.mult)\
                        .then_inc(*dv_s.done("qn", l, h))
                    dve.wait_ge(*pe_s.at("s", l, h))
                    dve.wait_ge(*po_s.at("wm", l, h))
                    if h >= 2:
                        dve.wait_ge(*pe_s.at("intra", l, h - 2))
                    nc.vector.tensor_tensor(s[:, 0:384], of(l, "s", h)[:, 0:384], w[:, 0:384], ALU.mult).then_inc(*dv_s.done())
                    nc.vector.tensor_tensor(s[0:NS, 384:448], of(l, "s", h)[0:NS, 384:448], w[0:NS, 384:448], ALU.mult)\
                        .then_inc(*free(dv_s, l, "s", h))
                    table[("dve", "sw", l, h)] = dv_s.count
                    for t, (t0, r) in enumerate(TT):
                        dve.wait_ge(*pe_s.at("ktB", l, h, t))
                        nc.vector.tensor_scalar(kTB[0:r, t, h * 256:(h + 1) * 256], of(l, "ktB", h, t)[0:r, 0:256],
                                                colA[0:r, t, 4 + h:5 + h], None, ALU.mult)\
                            .then_inc(*free(dv_s, l, "ktB", h, t))
                        table[("dve", "ktB", l, h, t)] = dv_s.count
                    dve.wait_ge(*pe_s.at("den", l, h))
                    nc.vector.scalar_tensor_tensor(rd[h % 2], of(l, "den", h)[:, 0:T], -1.0, eb[h % 2][:, 0:T],
                                                   ALU.mult, ALU.max).then_inc(*dv_s.done())
                    settle()
                    nc.vector.tensor_tensor(rd[h % 2], rd[h % 2], of(l, "den", h)[:, 0:T], ALU.max)\
                        .then_inc(*free(dv_s, l, "den", h))
                    settle()
                    nc.vector.reciprocal(rd[h % 2], rd[h % 2]).then_inc(*dv_s.done())
                    settle()
                    nc.vector.tensor_copy(rdS[:, h, :], rd[h % 2][:, SEQ:T]).then_inc(*dv_s.done())
                    nc.vector.tensor_tensor(hB[:, 2 * h:2 * h + 2, 0:SEQ],
                                            of(l, "num", h).rearrange("p (c t) -> p c t", c=2),
                                            rd[h % 2][:, 0:SEQ].unsqueeze(1).broadcast_to([P, 2, SEQ]), ALU.mult)\
                        .then_inc(*free(dv_s, l, "num", h))
                    nv = nS.rearrange("p (b h c) -> p h c b", b=DB, h=HB)[:, h]
                    dve.wait_ge(*pe_s.at("nn", l, h))
                    nc.vector.tensor_tensor(nv, n0v, eb[h % 2][:, T + NS:].unsqueeze(1).broadcast_to([P, 2, DB]), ALU.mult)\
                        .then_inc(*dv_s.done())
                    nc.vector.tensor_copy(nP[:, 2 * h:2 * h + 2], of(l, "nn", h)[:, 16:18]).then_inc(*dv_s.done())
                    settle()
                    nc.vector.tensor_tensor(nv, nv, of(l, "nn", h)[:, 0:16].rearrange("p (c b) -> p c b", c=2), ALU.add)\
                        .then_inc(*free(dv_s, l, "nn", h))
                    table[("dve", "nS", l, h)] = dv_s.count
                def hgrn_norm(h):
                    nc.vector.reciprocal(rsA[:, h, :], rsA[:, h, :]).then_inc(*dv_s.done())
                    settle()
                    nc.vector.scalar_tensor_tensor(oA[:, h, :], rsA[:, h, :], col("an", l, h), oA[:, h, :],
                                                   ALU.mult, ALU.mult).then_inc(*dv_s.done())
                    settle()
                    nc.vector.tensor_tensor(oA[:, h, :], oA[:, h, :], gS[:, h, :], ALU.mult).then_inc(*dv_s.done("oA", l))

                for b in range(DB):
                    c0 = strip_at(l, "C", b // 2)[0].rearrange("p (b h v) -> p b h v", b=2, h=HB)
                    dve.wait_ge(*pe_s.at("interB", l, b))
                    for h in range(HB):
                        dve.wait_ge(*pe_s.at("dC", l, b, h))
                        c = c0[:, b % 2, h, :]
                        nc.vector.scalar_tensor_tensor(c, c, decB[:, h, b:b + 1], of(l, "dC", b, h), ALU.mult, ALU.add)\
                            .then_inc(*free(dv_s, l, "dC", b, h))
                    table[("dve", "newC", l, b)] = dv_s.count
                    if b == 0:
                        dve.wait_ge(*ac_s.at("rsA", l))
                        dve.wait_ge(*ac_s.at("silu g", l))
                    hgrn_norm(b)
                dve.wait_ge(*pe_s.at("nS", l))
                nc.vector.tensor_tensor(hB[:, :, SEQ:T].rearrange("p (h c) t -> p h c t", h=HB),
                                        of(l, "nS").rearrange("p (h c t) -> p h c t", h=HB, c=2),
                                        rdS.unsqueeze(2).broadcast_to([P, HB, 2, NS]), ALU.mult)\
                    .then_inc(*free(dv_s, l, "nS"))
                table[("dve", "hB", l)] = dv_s.count
                for i in range(2):
                    for m in range(4):
                        dve.wait_ge(*pe_s.at("mm", l, "pa", i, m))
                        nc.vector.tensor_copy(yA[:, 4 * i + m, :], of(l, "pa", i, m)[:, 0:T]).then_inc(*free(dv_s, l, "pa", i, m))
                for h in range(HB):
                    dve.wait_ge(*pe_s.at("muB", l, h))
                    v = hB[:, 2 * h:2 * h + 2, :]
                    nc.vector.scalar_tensor_tensor(v, of(l, "muB", h)[:, 0:T].unsqueeze(1).broadcast_to([P, 2, T]),
                                                   -1.0 / 256, v, ALU.mult, ALU.add).then_inc(*free(dv_s, l, "muB", h))
                    table[("dve", "xcB", l, h)] = dv_s.count
                for m in range(KC):
                    dve.wait_ge(*ac_s.at("ga", l, m))
                    nc.vector.tensor_tensor(yA[:, m, :], yA[:, m, :], tg[m % 2], ALU.mult).then_inc(*dv_s.done("yA", l, m))
                dve.wait_ge(*ac_s.at("rsB", l))
                nc.vector.reciprocal(rsB[:, 0:HB, :], rsB[:, 0:HB, :]).then_inc(*dv_s.done())
                settle()
                for c in range(KC):
                    nc.vector.scalar_tensor_tensor(hB[:, c, :], rsB[:, c // 2, :], col("bn", l, c), hB[:, c, :],
                                                   ALU.mult, ALU.mult).then_inc(*dv_s.done())
                settle()
                dve.wait_ge(*ac_s.at("bo", l))
                nc.vector.tensor_tensor(hB, hB, boS, ALU.mult).then_inc(*dv_s.done("hBo", l))
                dve.wait_ge(*ac_s.at("gb", l))
                for m in range(KC):
                    dve.wait_ge(*pe_s.at("mm", l, "pb", m // 4, m % 4))
                    nc.vector.tensor_tensor(merged[:, m, :], of(l, "pb", m // 4, m % 4)[:, 0:T], gbS[:, m, :], ALU.mult)\
                        .then_inc(*free(dv_s, l, "pb", m // 4, m % 4))
                    settle()
                    nc.vector.tensor_tensor(merged[:, m, :], merged[:, m, :], yA[:, m, :], ALU.add)\
                        .then_inc(*dv_s.done("merged", l, m))
                for i in range(2):
                    for m in range(4):
                        k = 4 * i + m
                        dve.wait_ge(*pe_s.at("mm", l, "wo", i, m))
                        nc.vector.scalar_tensor_tensor(x1T[:, k, :], xT[:, k, :], ALPHA, of(l, "wo", i, m)[:, 0:T],
                                                       ALU.mult, ALU.add).then_inc(*free(dv_s, l, "wo", i, m))
                        table[("dve", "res1", l, k)] = dv_s.count
                norm(l, "1", x1T)
                if l % 2 == 0:
                    with dve.Fori(0, FC // 2) as i:
                        for s in range(2):
                            dve.wait_ge(ff_silu[s], i + 2)
                            dve.wait_ge(ff_up[s], i + 2)
                            nc.vector.tensor_tensor(hT[:, 2 * i + s, :], silu[s], bank[2 * s + 1][:, 0:T], ALU.mult)\
                                .then_inc(ff_h[s], 1)
                    with dve.Fori(0, KC // 2) as i:
                        for s in range(2):
                            dve.wait_ge(ff_down[s], i + 2)
                            nc.vector.scalar_tensor_tensor(x1T[:, 2 * i + s, :], x1T[:, 2 * i + s, :], ALPHA,
                                                           bank[4 + s][:, 0:T], ALU.mult, ALU.add).then_inc(ff_res[s], 1)
                    for s in range(2):
                        dve.wait_ge(ff_res[s], KC // 2 + 1)
                    norm(l, "2", x1T)
                else:
                    vector_moe(l)
                    norm(l, "2", acc)

        @block.gpsimd
        def _(pool):
            nc.gpsimd.memset(ident, 0.0).then_inc(*po_s.done())
            nc.gpsimd.memset(ones, 1.0).then_inc(*po_s.done())
            nc.gpsimd.memset(eps, EPS).then_inc(*po_s.done())
            nc.gpsimd.memset(keep, 1.0).then_inc(*po_s.done())
            nc.gpsimd.memset(drop, 0.0).then_inc(*po_s.done())
            pool.wait_ge(*po_s.last())
            nc.gpsimd.affine_select(out=ident, in_=ident, compare_op=ALU.not_equal, fill=1.0, base=0,
                                    pattern=[[-1, P]], channel_multiplier=1).then_inc(*po_s.done())
            for dst, v in ((keep, 0.0), (drop, NEG)):
                nc.gpsimd.memset(dst[:, 0:1], v).then_inc(*po_s.done())
                nc.gpsimd.memset(dst[:, SEQ:T:DS], v).then_inc(*po_s.done("ident"))
            nc.gpsimd.iota(rowI, pattern=[[0, P]], base=0, channel_multiplier=1).then_inc(*po_s.done())
            nc.gpsimd.iota(colI, pattern=[[1, P]], base=0, channel_multiplier=0).then_inc(*po_s.done("iota"))
            for l in range(DEPTH):
                if l > 0:
                    pool.wait_ge(*ac_s.at("ln2", l - 1, KC - 1))
                for t in (Qe[0], Qe[1], Ke[0], Ke[1]):
                    nc.gpsimd.memset(t, 0.0).then_inc(*po_s.done())
                for hf in range(2):
                    if hf == 1:
                        pool.wait_ge(*ac_s.at("exp end", l, 0))
                    nc.gpsimd.memset(R, 0.0).then_inc(*po_s.done("R", l, hf))
                    pool.wait_ge(*ac_s.at("log f", l, hf))
                    for lv in range(LEVELS):
                        h, n = 1 << lv, T if lv <= 2 else SEQ
                        rb, pb = blocks(R, h, n), blocks(fP[hf], h, n)
                        pool.wait_ge(*ac_s.at("exp", l, hf, lv))
                        pool.wait_ge(*po_s.last())
                        left, right = half(rb, 0, h), half(pb, 1, h)
                        nc.gpsimd.tensor_tensor(left, left, half(pb, 1, h, last=True).broadcast_to(left.shape), ALU.add)\
                            .then_inc(*po_s.done())
                        if lv < LEVELS - 1:
                            pool.wait_ge(*po_s.last())
                            nc.gpsimd.tensor_tensor(right, right, half(pb, 0, h, last=True).broadcast_to(right.shape), ALU.add)\
                                .then_inc(*po_s.done())
                        table[("pool", "update", l, hf, lv)] = po_s.count
                    if hf == 0:
                        pool.wait_ge(*dv_s.at("qS", l, 0))
                        pool.wait_ge(*ac_s.at("scT"))
                        nc.gpsimd.memset(U[:, :, 0:UP], 0.0).then_inc(*po_s.done())
                        nc.gpsimd.tensor_copy(U[:, :, UP + SEQ:].rearrange("p c (b u) -> p c b u", b=DB)[:, :, :, 0:UP],
                                              scT[:, :, 24 * l:24 * l + 24].rearrange("p c (b r) -> p c b r", b=DB))\
                            .then_inc(*po_s.done("U", l))
                pool.wait_ge(*ac_s.at("kt", l, 1, 2))
                pool.wait_ge(*dv_s.at("masks"))
                for b in range(DB):
                    if b >= 2:
                        pool.wait_ge(*pe_s.at("dS", l, b - 2, 1))
                    nc.gpsimd.tensor_scalar(kmA[b % 2], kTok[:, 2, :], seg[:, b:b + 1], None, ALU.mult)\
                        .then_inc(*po_s.done("kmA", l, b))
                for h in range(HB):
                    w = wW[h % 2]
                    pool.wait_ge(*ac_s.at("ew", l, h))
                    nc.gpsimd.tensor_tensor(w[:, 0:128], w[:, 0:128], causal, ALU.mult).then_inc(*po_s.done())
                    nc.gpsimd.tensor_tensor(w[:, 256:384], w[:, 256:384], causal, ALU.mult).then_inc(*po_s.done())
                    nc.gpsimd.tensor_tensor(w[0:NS, 384:448], w[0:NS, 384:448], own8[0:NS, :], ALU.mult)\
                        .then_inc(*po_s.done("wm", l, h))
                pool.wait_ge(*pe_s.at("kB", l, KC - 1))
                for i in range(2):
                    nc.gpsimd.memset(qz[i], 0.0).then_inc(*po_s.done())
                pool.wait_ge(*po_s.last())
                pool.wait_ge(*dv_s.at("ktB", l, HB - 1, 2))
                pool.wait_ge(*pe_s.at("rms", l, HA - 1))
                for b in range(DB):
                    if b >= 2:
                        pool.wait_ge(*pe_s.at("interB", l, b - 2))
                        nc.gpsimd.memset(qz[b % 2][:, :, (b - 2) * DS:(b - 1) * DS], 0.0).then_inc(*po_s.done())
                    nc.gpsimd.tensor_copy(qz[b % 2][:, :, b * DS:(b + 1) * DS], qI[:, :, b * DS:(b + 1) * DS])\
                        .then_inc(*po_s.done("qz", l, b))
                    if b >= 2:
                        pool.wait_ge(*pe_s.at("dC", l, b - 2, HB - 1))
                    nc.gpsimd.tensor_scalar(kmB[b % 2], kTB[:, 2, :], seg[:, b:b + 1], None, ALU.mult)\
                        .then_inc(*po_s.done("kmB", l, b))
            def experts(it0):
                with pool.Fori(0, NE // 2) as pr:
                    it = it0 + pr
                    for q in range(2 * EST):
                        ei, j = divmod(q, EST)
                        pool.wait_ge(mo_w2l[q % 2], it * EST + q // 2 + 1)
                        pool.dma_start(mo_w2[q % 2], I["w_ex_down"][0, bass.ds(2 * pr + ei, 1), j * NG:(j + 1) * NG, :]
                                       .rearrange("e (f p) n -> p (e f) n", p=P)).then_inc(moe_in2[q % 2], 16)

            pool.wait_ge(*pe_s.at("strip", 1, "wo", 1))
            pool.wait_ge(*pe_s.at("var1", 1))
            nc.gpsimd.memset(tri8, 1.0).then_inc(*po_s.done())
            pool.wait_ge(*po_s.last())
            nc.gpsimd.affine_select(out=tri8, in_=tri8, compare_op=ALU.is_gt, fill=0.0, base=0,
                                    pattern=[[1, NE], [-1, NE]], channel_multiplier=0).then_inc(*po_s.done("tri8"))
            nc.gpsimd.iota(iotaI, pattern=[[1, P]], base=0, channel_multiplier=0).then_inc(*po_s.done("moe"))
            experts(0)
            pool.wait_ge(*dv_s.at("pos"))
            flag = pool.value_load(over, min_val=0, max_val=1)
            with pool.If(flag > 0):
                with pool.Fori(1, 3) as ps:
                    experts(ps * (NE // 2))

        @block.sync
        def _(sp):
            def strip_src(l, name, i):
                if name == "S":
                    return I["state_hgrn"][l, 4 * i:4 * i + 4].rearrange("b h k v -> k b h v")
                if name == "C":
                    return I["state_mlstm_c"][l, 2 * i:2 * i + 2].rearrange("b h (c k) v -> k b h c v", c=2)
                w = I[MIX_OUT[name]][l] if name in MIX_OUT else I["w_in"][l]
                c0 = (0 if name in MIX_OUT else W_COL[name]) + 512 * i
                return w[:, c0:c0 + 512].rearrange("(k p) n -> p k n", p=P)

            def strip_dst(n, name):
                s = ring[:, n % RING, :]
                if name == "S":
                    return s.rearrange("p (b h v) -> p b h v", b=4, h=HA)
                if name == "C":
                    return s.rearrange("p (b h c v) -> p b h c v", b=2, h=HB, c=2)
                return s.rearrange("p (k n) -> p k n", k=KC)

            def released(l, name, i):
                if name in ("S", "C"):
                    sp.wait_ge(stored[f"{name}{i}"], 16 * (l + 1))
                else:
                    sp.wait_ge(*pe_s.at("strip", l, name, i))

            def load_strip(l, i):
                n = l * NSTRIP + i
                name, j = STRIPS[i]
                if i >= RING:
                    released(l, *STRIPS[i - RING])
                elif l > 0:
                    for s in range(2):
                        sp.wait_ge(*((ff_up[s], FC // 2 + 1) if i == 0 else (ff_down[s], KC // 2 + 1)))
                src, dst = strip_src(l, name, j), strip_dst(n, name)
                sp.dma_start(dst, src).then_inc(ring_full[n % RING], 16)

            def store_states(l, name, i):
                n = l * NSTRIP + STRIPS.index((name, i))
                out = O["hgrn_sample"][l, 4 * i:4 * i + 4].rearrange("b h k v -> k b h v") if name == "S" else \
                    O["c_sample"][l, 2 * i:2 * i + 2].rearrange("b h (c k) v -> k b h c v", c=2)
                last = 4 * i + 3 if name == "S" else 2 * i + 1
                sp.wait_ge(*dv_s.at("newS" if name == "S" else "newC", l, last))
                sp.dma_start(out, strip_dst(n, name)).then_inc(stored[f"{name}{i}"], 16)

            def experts(it0):
                with sp.Fori(0, NE // 2) as pr:
                    it = it0 + pr
                    for q in range(2 * EST):
                        ei, j = divmod(q, EST)
                        sp.wait_ge(mo_w1l[q % 2], it * EST + q // 2 + 1)
                        for g, w in enumerate((I["w_ex_gate"], I["w_ex_up"])):
                            sp.dma_start(mo_w1[q % 2].rearrange("p k (g n) -> p g k n", g=2)[:, g],
                                         w[0, bass.ds(2 * pr + ei, 1), :, j * NG:(j + 1) * NG]
                                         .rearrange("e (k p) n -> p (e k) n", p=P)).then_inc(moe_in[q % 2], 16)

            def store_prompt(l, hf):
                sp.wait_ge(*ac_s.at("st", l, hf))
                sp.dma_start(O["hgrn_prompt"][l, 0, 4 * hf:4 * hf + 4].rearrange("h k v -> k h v"), stP)\
                    .then_inc(stored["st"], 16)

            def store_heads(l):
                sp.wait_ge(*dv_s.at("mout", l))
                sp.dma_start(O["m_sample"][l].rearrange("b h -> h b"), mout[:, 0:DB]).then_inc(stored["m"], 16)
                sp.dma_start(O["m_prompt"][l].rearrange("b h -> h b"), mout[:, DB:DB + 1]).then_inc(stored["m"], 16)
                sp.wait_ge(*ac_s.at("cvo", l))
                sp.dma_start(O["conv_prompt"][l, 0], cvo[0:UP, :]).then_inc(stored["conv"], 16)
                sp.dma_start(O["conv_sample"][l].rearrange("b r d -> (b r) d"), cvo[UP:27, :]).then_inc(stored["conv"], 16)
                for h in range(HB):
                    sp.wait_ge(*ac_s.at("cPo", l, h))
                    sp.dma_start(O["c_prompt"][l, 0, h].rearrange("(c k) v -> k c v", c=2), cP).then_inc(stored["cp"], 16)

            sp.dma_start(e_x[:, 0:2, :], I["x_prompt"][0].rearrange("(t p) d -> p t d", p=P)).then_inc(load["x"], 16)
            sp.dma_start(e_x[0:NS, 2, :], I["x_sample"].rearrange("b t d -> (b t) d")).then_inc(load["x"], 16)
            load_strip(0, 0)
            sp.dma_start(wr, I["w_router"][0].rearrange("(k p) e -> p k e", p=P)).then_inc(load["router"], 16)
            sp.dma_start(brt, I["b_router"][0].partition_broadcast(P)).then_inc(load["router"], 16)
            for name, src in (("lb", "lb_param"), ("an", "a_norm_g"), ("cb", "conv_b"), ("bn", "b_norm_g"),
                              ("g1", "ln1_g"), ("b1", "ln1_b"), ("g2", "ln2_g"), ("b2", "ln2_b")):
                sp.dma_start(e_par[PAR[name]:PAR[name] + 2, :], I[src]).then_inc(load["par"], 16)
            sp.dma_start(e_par[PAR["cw"]:PAR["cw"] + 8, :], I["conv_w"].rearrange("l j d -> (l j) d")).then_inc(load["par"], 16)
            sp.dma_start(e_conv, I["state_conv"].rearrange("l b r d -> (l b r) d")).then_inc(load["conv"], 16)
            for l in range(DEPTH):
                if l > 0:
                    sp.wait_ge(*pe_s.at("gate", l - 1, 1))
                    sp.wait_ge(*ac_s.at("n0T", l - 1))
                    sp.wait_ge(*dv_s.at("bd", l - 1))
                sp.dma_start(n0row, I["state_mlstm_n"][l].rearrange("b h (c d) -> (b h c) d", c=2)).then_inc(load["n0"], 16)
                sp.dma_start(gw, I["w_in"][l, :, C_BG:C_BG + 8].rearrange("(k p) n -> p k n", p=P)).then_inc(load["gates"], 16)
                sp.dma_start(wq4, I["w_q_blk"][l].rearrange("(c n) i j -> (n i) c j", c=KC)).then_inc(load["w4"], 16)
                sp.dma_start(wk4, I["w_k_blk"][l].rearrange("(c n) i j -> (n i) c j", c=KC)).then_inc(load["w4"], 16)
                for i in range(NSTRIP):
                    if l == 0 and i == 0:
                        continue
                    if i == 9:
                        store_prompt(l, 0)
                    if i == 15:
                        store_prompt(l, 1)
                    if i == 17:
                        store_heads(l)
                    if i >= RING and STRIPS[i - RING][0] in ("S", "C"):
                        store_states(l, *STRIPS[i - RING])
                    load_strip(l, i)
                sp.wait_ge(*ac_s.at("nro", l))
                sp.dma_start(O["n_sample"][l].rearrange("b h (c d) -> (b h c) d", c=2), nrow).then_inc(stored["n"], 16)
                sp.dma_start(O["n_prompt"][l, 0].rearrange("h (c d) -> (h c) d", c=2), nrowP).then_inc(stored["n"], 16)
                if l % 2 == 0:
                    for i in range(2):
                        sp.wait_ge(*pe_s.at("strip", l, "pb", i))
                    w1 = [I["w_ff_gate"][0], I["w_ff_up"][0]]
                    with sp.Fori(0, FC // 2) as i:
                        for s in range(2):
                            sp.wait_ge(ff_up[s], i + 1)
                            for g in range(2):
                                sp.dma_start(ff_w1[s][:, g], w1[g].rearrange("(k p) (i n) -> p i k n", p=P, n=P)[:, 2 * i + s])\
                                    .then_inc(ff_in[s], 16)
                    sp.wait_ge(*pe_s.at("strip", l, "wo", 1))
                    with sp.Fori(0, KC // 2) as i:
                        for s in range(2):
                            sp.wait_ge(ff_down[s], i + 1)
                            sp.dma_start(ff_w2[s], I["w_ff_down"][0].rearrange("(f p) (i n) -> p i f n", p=P, n=P)[:, 2 * i + s])\
                                .then_inc(ff_in2[s], 16)
                else:
                    sp.wait_ge(*pe_s.at("strip", l, "wo", 1))
                    experts(0)
                    sp.wait_ge(*dv_s.at("pos"))
                    flag = sp.value_load(over, min_val=0, max_val=1)
                    with sp.If(flag > 0):
                        with sp.Fori(1, 3) as ps:
                            experts(ps * (NE // 2))
            sp.wait_ge(*ac_s.at("y"))
            sp.dma_start(O["y_prompt"][0].rearrange("(t p) d -> p t d", p=P), yrow[:, 0:2, :]).then_inc(stored["y"], 16)
            sp.dma_start(O["y_sample"].rearrange("b t d -> (b t) d"), yrow[0:NS, 2, :]).then_inc(stored["y2"], 16)
            sp.wait_ge(stored["y"], 16)
            sp.wait_ge(stored["y2"], 16)
            for name in ("S0", "S1", "C0", "C1", "C2", "C3"):
                sp.wait_ge(stored[name], 16 * DEPTH)
            sp.wait_ge(stored["st"], 32 * DEPTH)
            sp.wait_ge(stored["cp"], 16 * HB * DEPTH)
            for name in ("conv", "n", "m"):
                sp.wait_ge(stored[name], 32 * DEPTH)


_INS = ["x_prompt", "x_sample", "state_hgrn", "state_mlstm_c", "state_mlstm_n", "state_mlstm_m", "state_conv",
        "w_in", "lb_param", "a_norm_g", "w_pa", "conv_w", "conv_b", "w_q_blk", "w_k_blk", "b_ig", "b_fg",
        "b_norm_g", "w_pb", "w_o", "ln1_g", "ln1_b", "ln2_g", "ln2_b", "w_ff_gate", "w_ff_up", "w_ff_down",
        "w_router", "b_router", "w_ex_gate", "w_ex_up", "w_ex_down"]
_OUTS = [("y_prompt", (1, SEQ, D)), ("y_sample", (DB, DS, D)),
         ("hgrn_prompt", (DEPTH, 1, HA, P, P)), ("hgrn_sample", (DEPTH, DB, HA, P, P)),
         ("c_prompt", (DEPTH, 1, HB, 256, 256)), ("c_sample", (DEPTH, DB, HB, 256, 256)),
         ("n_prompt", (DEPTH, 1, HB, 256)), ("n_sample", (DEPTH, DB, HB, 256)),
         ("m_prompt", (DEPTH, 1, HB)), ("m_sample", (DEPTH, DB, HB)),
         ("conv_prompt", (DEPTH, 1, UP, D)), ("conv_sample", (DEPTH, DB, UP, D))]


def _declare(nc, arrays):
    ins = {n: nc.dram_tensor(f"in_{n}", a.shape, mybir.dt.from_np(a.dtype), kind="ExternalInput").ap()
           for n, a in arrays.items()}
    outs = {n: nc.dram_tensor(f"out_{n}", shape, F32, kind="ExternalOutput").ap() for n, shape in _OUTS}
    return ins, outs


def kernel(**inputs):
    import numpy as _np
    import concourse.bacc as _bacc
    from concourse.bass_utils import run_bass_kernel_spmd as _run

    arrays = {n: _np.ascontiguousarray(inputs[n]) for n in _INS}
    table = {}
    for _ in range(2):
        nc = _bacc.Bacc("TRN2", target_bir_lowering=False, num_devices=1)
        build(nc, *_declare(nc, arrays), table)
        table["counted"] = True
    r = _run(nc, [{f"in_{n}": a for n, a in arrays.items()}], core_ids=[0])
    return tuple(r.results[0][f"out_{n}"] for n, _ in _OUTS)
```
